# Optimizing a Trainium2 kernel written in Bass

```python
import jax
import jax.numpy as jnp
from jax import lax
import numpy as np

D_MODEL = 1024
BATCH = 1
SEQ = 1024
DEPTH = 1
DEC_BATCH = 8
DEC_SEQ = 8
PAST_LEN = 1024
PAGE_SIZE = 128

ATTN_GROUPS = ((128, 1), (512, 4), (2048, 16))
N_ATTN_GROUPS = len(ATTN_GROUPS)
HEADS_PER_GROUP = 8
HEAD_DIM = 64
A_WIDTH = HEADS_PER_GROUP * HEAD_DIM
ATTN_SCALE = HEAD_DIM ** -0.5

SSD_EXPAND = 2
D_INNER = SSD_EXPAND * D_MODEL
SSD_HEAD_DIM = 64
SSD_HEADS = D_INNER // SSD_HEAD_DIM
SSD_GROUPS = 4
SSD_HEADS_PER_GROUP = SSD_HEADS // SSD_GROUPS
SSD_STATE = 128
CONV_W = 4
CONV_DIM = D_INNER + 2 * SSD_GROUPS * SSD_STATE
SSD_CHUNK = 128

D_FF = ((8 * D_MODEL + 3 * 256 - 1) // (3 * 256)) * 256

N_IN = 3 * N_ATTN_GROUPS * A_WIDTH + D_INNER + CONV_DIM + SSD_HEADS + 2 * D_MODEL
RMS_EPS = 1e-6

kernel_name = 'hybrid_dilated_attn_ssd_step'

def rmsnorm(x, w):
    xf = x.astype(jnp.float32)
    y = xf * lax.rsqrt(jnp.mean(xf * xf, axis=-1, keepdims=True) + RMS_EPS)
    return (y * w.astype(jnp.float32)).astype(x.dtype)

def gated_group_rmsnorm(y, z, w):
    g = y.astype(jnp.float32) * jax.nn.silu(z.astype(jnp.float32))
    shp = g.shape
    g = g.reshape(shp[:-1] + (SSD_GROUPS, shp[-1] // SSD_GROUPS))
    g = g * lax.rsqrt(jnp.mean(g * g, axis=-1, keepdims=True) + RMS_EPS)
    return (g.reshape(shp) * w.astype(jnp.float32)).astype(y.dtype)

def split_in(u):
    lead = u.shape[:-1]
    heads = lambda t: t.reshape(lead + (HEADS_PER_GROUP, HEAD_DIM))
    qkv = []
    off = 0
    for _ in range(N_ATTN_GROUPS):
        q = heads(u[..., off:off + A_WIDTH])
        k = heads(u[..., off + A_WIDTH:off + 2 * A_WIDTH])
        v = heads(u[..., off + 2 * A_WIDTH:off + 3 * A_WIDTH])
        qkv.append((q, k, v))
        off += 3 * A_WIDTH
    z = u[..., off:off + D_INNER]
    off += D_INNER
    xbc = u[..., off:off + CONV_DIM]
    off += CONV_DIM
    dt_raw = u[..., off:off + SSD_HEADS]
    off += SSD_HEADS
    gate_raw = u[..., off:off + 2 * D_MODEL]
    return qkv, z, xbc, dt_raw, gate_raw

def masked_softmax_stats(s, valid):
    s = jnp.where(valid, s, -jnp.inf)
    m = jnp.max(s, axis=-1, keepdims=True)
    p = jnp.exp(s - m)
    den = jnp.sum(p, axis=-1, keepdims=True)
    return p / den, (m + jnp.log(den))[..., 0]

def dilated_attn_prompt(q, k, v, window, dil):
    b, l, h, e = q.shape
    band = window // dil
    span = dil * band
    lp = -(-l // span) * span
    nb = lp // span

    def to_blocks(t):
        t = jnp.pad(t, ((0, 0), (0, lp - l), (0, 0), (0, 0)))
        t = t.reshape(b, lp // dil, dil, h, e).transpose(0, 2, 1, 3, 4)
        return t.reshape(b, dil, nb, band, h, e)

    def with_prev(t):
        prev = jnp.pad(t, ((0, 0), (0, 0), (1, 0), (0, 0), (0, 0), (0, 0)))[:, :, :-1]
        return jnp.concatenate([prev, t], axis=3)

    qb = to_blocks(q)
    kk = with_prev(to_blocks(k))
    vv = with_prev(to_blocks(v))
    s = jnp.einsum('brnqhe,brnkhe->brnhqk', qb, kk).astype(jnp.float32) * ATTN_SCALE
    qi = jnp.arange(band)[:, None]
    ki = jnp.arange(2 * band)[None, :]
    dist = qi + band - ki
    band_ok = (dist >= 0) & (dist <= band)
    blk = jnp.arange(nb)[:, None, None]
    valid = band_ok[None] & ((blk > 0) | (ki[None] >= band))
    p, lse = masked_softmax_stats(s, valid[None, None, :, None])
    o = jnp.einsum('brnhqk,brnkhe->brnqhe', p.astype(v.dtype), vv)
    lse = lse.transpose(0, 1, 2, 4, 3)

    def from_blocks(t):
        t = t.reshape((b, dil, lp // dil) + t.shape[4:])
        t = jnp.moveaxis(t, 1, 2).reshape((b, lp) + t.shape[3:])
        return t[:, :l]

    return from_blocks(o), from_blocks(lse)

def dilated_attn_sample(q, kv_all, past_rows, window, dil):
    b, s_len, h, e = q.shape
    nk = window // dil + 1
    idx = past_rows + jnp.arange(s_len)[:, None] - dil * jnp.arange(nk)[None, :]
    valid = idx >= 0
    g = jnp.take(kv_all, jnp.maximum(idx, 0).reshape(-1), axis=1).reshape(b, s_len, nk, 2, h, e)
    s = jnp.einsum('bshe,bskhe->bshk', q, g[:, :, :, 0]).astype(jnp.float32) * ATTN_SCALE
    p, lse = masked_softmax_stats(s, valid[None, :, None, :])
    o = jnp.einsum('bshk,bskhe->bshe', p.astype(q.dtype), g[:, :, :, 1])
    return o, lse

def merge_dilation_groups(outs, lses):
    w = jax.nn.softmax(jnp.stack(lses, axis=0), axis=0)
    o = jnp.einsum('gblh,gblhe->blhe', w, jnp.stack(outs, axis=0).astype(jnp.float32))
    return o.reshape(o.shape[:2] + (A_WIDTH,))

def ssd_chunked(x, dt, a, bm, cm, s0):
    b, l = x.shape[:2]
    q = min(SSD_CHUNK, l)
    lp = -(-l // q) * q
    nc = lp // q

    def chunks(t):
        t = jnp.pad(t.astype(jnp.float32), ((0, 0), (0, lp - l)) + ((0, 0),) * (t.ndim - 2))
        return jnp.moveaxis(t.reshape((b, nc, q) + t.shape[2:]), 1, 0)

    xs = (chunks(x), chunks(dt), chunks(bm), chunks(cm))
    causal = jnp.tril(jnp.ones((q, q), dtype=bool))

    def step(s, inp):
        xc, dtc, bc, cc = inp
        cum = jnp.cumsum(dtc * a, axis=1)
        seg = cum[:, :, None] - cum[:, None, :]
        decay = jnp.exp(jnp.where(causal[None, :, :, None, None], seg, -jnp.inf))
        cb = jnp.einsum('btgn,bsgn->btsg', cc, bc)
        w = cb[..., None] * decay * dtc[:, None]
        y = jnp.einsum('btsgh,bsghp->btghp', w, xc)
        y = y + jnp.einsum('btgn,bghpn->btghp', cc, s) * jnp.exp(cum)[..., None]
        to_end = jnp.exp(cum[:, -1:] - cum) * dtc
        s = jnp.exp(cum[:, -1])[..., None, None] * s + jnp.einsum('bsgh,bsghp,bsgn->bghpn', to_end, xc, bc)
        return s, y

    s_fin, ys = lax.scan(step, s0.astype(jnp.float32), xs)
    y = jnp.moveaxis(ys, 0, 1).reshape((b, lp) + x.shape[2:])[:, :l]
    return y, s_fin

def layer(x, kv_past, conv_prev, ssm_prev, p):
    b, l, _ = x.shape
    h = rmsnorm(x, p['pre_mix_norm'])
    u = h @ p['w_in']
    qkv, z, xbc, dt_raw, gate_raw = split_in(u)

    outs, lses, new_kv = [], [], []
    for gi, (window, dil) in enumerate(ATTN_GROUPS):
        q, k, v = qkv[gi]
        kv_new = jnp.stack([k, v], axis=2)
        if kv_past is None:
            o, lse = dilated_attn_prompt(q, k, v, window, dil)
            keep = min(window, l)
            new_kv.append(kv_new[:, l - keep:])
        else:
            past = kv_past[gi].astype(kv_new.dtype)
            rows = past.shape[1]
            kv_all = jnp.concatenate([past, kv_new], axis=1)
            o, lse = dilated_attn_sample(q, kv_all, rows, window, dil)
            new_kv.append(kv_all[:, kv_all.shape[1] - rows:])
        outs.append(o)
        lses.append(lse)
    a_out = merge_dilation_groups(outs, lses).astype(x.dtype)

    conv_in = jnp.concatenate([conv_prev.astype(x.dtype), xbc], axis=1)
    conv = p['conv_b']
    for i in range(CONV_W):
        conv = conv + conv_in[:, i:i + l] * p['conv_w'][i]
    conv = jax.nn.silu(conv)
    new_conv = conv_in[:, conv_in.shape[1] - (CONV_W - 1):]
    xs = conv[..., :D_INNER].reshape(b, l, SSD_GROUPS, SSD_HEADS_PER_GROUP, SSD_HEAD_DIM)
    bm = conv[..., D_INNER:D_INNER + SSD_GROUPS * SSD_STATE].reshape(b, l, SSD_GROUPS, SSD_STATE)
    cm = conv[..., D_INNER + SSD_GROUPS * SSD_STATE:].reshape(b, l, SSD_GROUPS, SSD_STATE)
    dt = jax.nn.softplus(dt_raw.astype(jnp.float32) + p['dt_bias'].astype(jnp.float32))
    dt = dt.reshape(b, l, SSD_GROUPS, SSD_HEADS_PER_GROUP)
    a = -jnp.exp(p['a_log'].astype(jnp.float32)).reshape(SSD_GROUPS, SSD_HEADS_PER_GROUP)
    s0 = ssm_prev.reshape(b, SSD_GROUPS, SSD_HEADS_PER_GROUP, SSD_HEAD_DIM, SSD_STATE)
    y, s_new = ssd_chunked(xs, dt, a, bm, cm, s0)
    d_skip = p['d_skip'].astype(jnp.float32).reshape(SSD_GROUPS, SSD_HEADS_PER_GROUP)
    y = y + d_skip[:, :, None] * xs.astype(jnp.float32)
    y = gated_group_rmsnorm(y.reshape(b, l, D_INNER).astype(x.dtype), z, p['ssd_norm'])

    a_proj = a_out @ p['w_attn_out']
    b_proj = y @ p['w_ssd_out']
    gate_a = jax.nn.sigmoid(gate_raw[..., :D_MODEL])
    gate_b = jax.nn.sigmoid(gate_raw[..., D_MODEL:])
    mixed = (gate_a * a_proj + gate_b * b_proj) @ p['w_out']
    x = x + rmsnorm(mixed, p['post_mix_norm'])

    h2 = rmsnorm(x, p['pre_ffn_norm'])
    gu = h2 @ p['w_up']
    f = (jax.nn.silu(gu[..., :D_FF]) * gu[..., D_FF:]) @ p['w_down']
    x = x + rmsnorm(f, p['post_ffn_norm'])

    ssm_out = s_new.reshape(b, SSD_HEADS, SSD_HEAD_DIM, SSD_STATE).astype(x.dtype)
    return x, new_kv, new_conv, ssm_out

def setup_inputs(seed: int = 0) -> dict:
    key = jax.random.key(seed)
    ks = jax.random.split(key, 26)
    f32 = jnp.float32
    nrm = lambda k, shape, scale: jax.random.normal(k, shape, f32) * scale
    kv_shape = lambda w: (DEPTH, DEC_BATCH, min(w, PAST_LEN), 2, HEADS_PER_GROUP, HEAD_DIM)
    dt0 = jnp.exp(jax.random.uniform(ks[9], (DEPTH, SSD_HEADS), f32, np.log(1e-3), np.log(1e-1)))
    return {
        'x_prompt': nrm(ks[0], (BATCH, SEQ, D_MODEL), 1.0),
        'x_sample': nrm(ks[1], (DEC_BATCH, DEC_SEQ, D_MODEL), 1.0),
        'cache_kv_w128': nrm(ks[2], kv_shape(ATTN_GROUPS[0][0]), 1.0),
        'cache_kv_w512': nrm(ks[3], kv_shape(ATTN_GROUPS[1][0]), 1.0),
        'cache_kv_w2048': nrm(ks[4], kv_shape(ATTN_GROUPS[2][0]), 1.0),
        'state_conv': nrm(ks[5], (DEPTH, DEC_BATCH, CONV_W - 1, CONV_DIM), 1.0),
        'state_ssm': nrm(ks[6], (DEPTH, DEC_BATCH, SSD_HEADS, SSD_HEAD_DIM, SSD_STATE), 0.5),
        'pre_mix_norm': 1.0 + nrm(ks[7], (DEPTH, D_MODEL), 0.05),
        'w_in': nrm(ks[8], (DEPTH, D_MODEL, N_IN), D_MODEL ** -0.5),
        'conv_w': nrm(ks[10], (DEPTH, CONV_W, CONV_DIM), CONV_W ** -0.5),
        'conv_b': nrm(ks[11], (DEPTH, CONV_DIM), 0.02),
        'dt_bias': dt0 + jnp.log(-jnp.expm1(-dt0)),
        'a_log': jnp.log(jax.random.uniform(ks[12], (DEPTH, SSD_HEADS), f32, 1.0, 16.0)),
        'd_skip': 1.0 + nrm(ks[13], (DEPTH, SSD_HEADS), 0.1),
        'ssd_norm': 1.0 + nrm(ks[14], (DEPTH, D_INNER), 0.05),
        'w_attn_out': nrm(ks[15], (DEPTH, A_WIDTH, D_MODEL), A_WIDTH ** -0.5),
        'w_ssd_out': nrm(ks[16], (DEPTH, D_INNER, D_MODEL), D_INNER ** -0.5),
        'w_out': nrm(ks[17], (DEPTH, D_MODEL, D_MODEL), D_MODEL ** -0.5),
        'post_mix_norm': 1.0 + nrm(ks[18], (DEPTH, D_MODEL), 0.05),
        'pre_ffn_norm': 1.0 + nrm(ks[19], (DEPTH, D_MODEL), 0.05),
        'w_up': nrm(ks[20], (DEPTH, D_MODEL, 2 * D_FF), D_MODEL ** -0.5),
        'w_down': nrm(ks[21], (DEPTH, D_FF, D_MODEL), D_FF ** -0.5),
        'post_ffn_norm': 1.0 + nrm(ks[22], (DEPTH, D_MODEL), 0.05),
    }

def reference(x_prompt, x_sample, cache_kv_w128, cache_kv_w512, cache_kv_w2048, state_conv, state_ssm,
              pre_mix_norm, w_in, conv_w, conv_b, dt_bias, a_log, d_skip, ssd_norm,
              w_attn_out, w_ssd_out, w_out, post_mix_norm, pre_ffn_norm, w_up, w_down, post_ffn_norm):
    yp, ys = x_prompt, x_sample
    pk0, pk1, pk2, pconv, pssm = [], [], [], [], []
    sk0, sk1, sk2, sconv, sssm = [], [], [], [], []
    for li in range(DEPTH):
        p = {
            'pre_mix_norm': pre_mix_norm[li], 'w_in': w_in[li], 'conv_w': conv_w[li], 'conv_b': conv_b[li],
            'dt_bias': dt_bias[li], 'a_log': a_log[li], 'd_skip': d_skip[li], 'ssd_norm': ssd_norm[li],
            'w_attn_out': w_attn_out[li], 'w_ssd_out': w_ssd_out[li], 'w_out': w_out[li],
            'post_mix_norm': post_mix_norm[li], 'pre_ffn_norm': pre_ffn_norm[li], 'w_up': w_up[li],
            'w_down': w_down[li], 'post_ffn_norm': post_ffn_norm[li],
        }
        b_p = yp.shape[0]
        conv0 = jnp.zeros((b_p, CONV_W - 1, CONV_DIM), yp.dtype)
        ssm0 = jnp.zeros((b_p, SSD_HEADS, SSD_HEAD_DIM, SSD_STATE), jnp.float32)
        yp, kvp, cvp, smp = layer(yp, None, conv0, ssm0, p)
        past = (cache_kv_w128[li], cache_kv_w512[li], cache_kv_w2048[li])
        ys, kvs, cvs, sms = layer(ys, past, state_conv[li], state_ssm[li], p)
        pk0.append(kvp[0]); pk1.append(kvp[1]); pk2.append(kvp[2]); pconv.append(cvp); pssm.append(smp)
        sk0.append(kvs[0]); sk1.append(kvs[1]); sk2.append(kvs[2]); sconv.append(cvs); sssm.append(sms)
    kv_w128_prompt = jnp.stack(pk0, axis=0)
    kv_w512_prompt = jnp.stack(pk1, axis=0)
    kv_w2048_prompt = jnp.stack(pk2, axis=0)
    conv_prompt = jnp.stack(pconv, axis=0)
    ssm_prompt = jnp.stack(pssm, axis=0)
    kv_w128_sample = jnp.stack(sk0, axis=0)
    kv_w512_sample = jnp.stack(sk1, axis=0)
    kv_w2048_sample = jnp.stack(sk2, axis=0)
    conv_sample = jnp.stack(sconv, axis=0)
    ssm_sample = jnp.stack(sssm, axis=0)
    return (yp, ys, kv_w128_prompt, kv_w512_prompt, kv_w2048_prompt, conv_prompt, ssm_prompt,
            kv_w128_sample, kv_w512_sample, kv_w2048_sample, conv_sample, ssm_sample)


_drawn_inputs = setup_inputs


def setup_inputs(seed=0):
    import zlib

    import numpy as np

    out = dict(_drawn_inputs(seed))
    spreads = {}
    factors = {}
    for name, (base, spread) in spreads.items():
        noise = np.random.default_rng([zlib.crc32(name.encode()), seed]).standard_normal(out[name].shape)
        drawn = base * np.exp(spread * noise) if base else spread * noise
        out[name] = jnp.asarray(drawn.astype(out[name].dtype))
    for name, factor in factors.items():
        out[name] = (out[name] * factor).astype(out[name].dtype)
    return out
```

```python
from contextlib import ExitStack

import concourse.bass as bass
from concourse import mybir

ACT = mybir.ActivationFunctionType
ALU = mybir.AluOpType
AX = mybir.AxisListType
F32 = mybir.dt.float32
F32R = mybir.dt.float32r
ds = bass.ds

P = 128
D = 1024
KD = D // P
SEQ = 1024
DB, DS = 8, 8
NS = DB * DS
T = SEQ + NS
NT = SEQ // P
PAST = 1024
HEADS, E_ = 8, 64
AW = HEADS * E_
ASC = E_ ** -0.5
GROUPS = ((128, 1), (512, 4), (2048, 16))
ROWS = tuple(min(w, PAST) for w, _ in GROUPS)
NG = len(GROUPS)
NJ = AW // P
DI = 2 * D
SG = 4
SH = 32
HG = SH // SG
NST = 128
XT = DI // SG // P
CONVD = DI + 2 * SG * NST
CT = CONVD // P
CW = 4
FF = 2816
FT = FF // P
Z0 = 3 * NG * AW
XBC0 = Z0 + DI
DT0 = XBC0 + CONVD
GATE0 = DT0 + SH
EPS = 1e-6
NEG = -1e30
TH = ((0, 368), (368, 736), (736, T))
PW = CW - 1 + SEQ
SW = CW - 1 + DS
CWID = PW + DB * SW

U_NORM0 = 1
U_DT = 2
U_SSD = 2
SSD_USES = 2 + 2 * XT + 1 + KD
U_ATT = U_SSD + SG * SSD_USES
U_SAM = U_ATT + NJ * NG * 3
U_PROJ = U_SAM + 3 * DB
U_OUT = U_PROJ + KD
U_NORME = U_OUT + KD + 1
U_NORMF = U_NORME + 1
U_FF = U_NORMF
FF_USES = 4 + KD
U_NORML = U_FF + (FT // 2) * FF_USES + 1
C_DT = 0
C_SSD = 1
SSD_CH = 2 + 2 * XT + KD
C_ATT = C_SSD + SG * SSD_CH
C_GATE = C_ATT + NJ * NG * 3
C_PROJ = C_GATE + 2 * KD
C_OUT = C_PROJ + KD
C_FF = C_OUT + KD
RAW, SPL = 2, 3


def trunk(nc, x_prompt, x_sample, cache0, cache1, cache2, state_conv, state_ssm, pre_mix_norm, w_in,
          conv_w, conv_b, dt_bias, a_log, d_skip, ssd_norm, w_attn_out, w_ssd_out, w_out,
          post_mix_norm, pre_ffn_norm, w_up, w_down, post_ffn_norm,
          y_prompt, y_sample, kvp0, kvp1, kvp2, conv_p, ssm_p, kvs0, kvs1, kvs2, conv_s, ssm_s):
    caches, kvp, kvs = (cache0, cache1, cache2), (kvp0, kvp1, kvp2), (kvs0, kvs1, kvs2)
    ctx = ExitStack()
    with ctx:
        def scratch(name, shape):
            return nc.dram_tensor(name, shape, F32, kind="Internal").ap()

        def sem(name):
            return ctx.enter_context(nc.semaphore(name))

        xt_scr = scratch("xt_scr", [P, KD, T])
        ba_scr = scratch("ba_scr", [P, KD, T])
        cum_scr = scratch("cum_scr", [SH, T])
        tok_scr = scratch("tok_scr", [P, SG, 9 * 4 * HG])
        cc_scr = scratch("cc_scr", [P, CT, 29])
        nc_scr = scratch("nc_scr", [CT, P, 27])
        gate_scr = scratch("gate_scr", [2, KD, P, T])
        o_scr = scratch("o_scr", [NJ, NG, SEQ, 132])
        mk_scr = scratch("mk_scr", [8, 1176])

        base = [1152]

        def at(name, shape, dt=F32, off=None):
            n = 4
            for s in shape[1:]:
                n *= s
            if off is None:
                off = base[0]
                base[0] += (n + 31) // 32 * 32
            return nc.alloc_sbuf_tensor_at(name, shape, dt, offset=off)

        H0 = base[0]
        hH = at("hH", [P, KD, T], F32R)
        hL = at("hL", [P, KD, T], F32R)
        wraw = [at(f"wraw{i}", [P, 1024]) for i in range(RAW)]
        wH = [at(f"wH{i}", [P, 1024], F32R) for i in range(SPL)]
        wL = [at(f"wL{i}", [P, 1024], F32R) for i in range(SPL)]
        ident = at("ident", [P, P])
        ones = at("ones", [P, P])
        smask = at("smask", [P, P])
        smaskS = at("smaskS", [NS, NS])
        bmask = at("bmask", [NS, DB])
        nrm = at("nrm", [P, 48])
        eps = at("eps", [P, 1])
        ecl = at("ecl", [P, 16, DB])
        dsk = at("dsk", [P, 16])
        tokg = at("tokg", [P, 9, 4, HG])
        ccg = at("ccg", [P, 6, 29])
        ncg = at("ncg", [P, 6, 27])
        elg = at("elg", [P, 2, HG])
        small = at("small", [P, 128])
        R1 = base[0]
        base[0] += KD * T * 4
        X0 = base[0]
        base[0] += KD * T * 4
        X1 = base[0]
        base[0] += 2 * XT * T * 4
        T0 = base[0]
        base[0] += 3 * T * 4
        assert base[0] <= nc.sbuf_usable_end, base[0]

        def region(start, name, items):
            out, o = [], start
            for nm, shape, dt in items:
                out.append(at(name + nm, shape, dt, off=o))
                n = 4
                for s in shape[1:]:
                    n *= s
                o += (n + 31) // 32 * 32
            return out, o

        acc8 = at("acc8", [P, KD, T], off=X0)
        (xin,), _ = region(X1, "p0", [("xin", [P, NT, D], F32)])
        (xins, rows48, convrows, strows), _ = region(R1, "p0", [
            ("xins", [NS, D], F32), ("rows48", [48, P], F32), ("convrows", [5, CONVD], F32), ("strows", [24, CONVD], F32)])
        (dtsel, dv, de, du, dl, dr, dcum), o = region(X1, "dt", [
            ("sel", [SH, 16, P], F32)] + [(n, [SH, T], F32) for n in ("v", "e", "u", "l", "r", "c")])
        assert o <= T0
        (tokd, ccd), o = region(R1 + 4096, "dt", [("tok", [P, SG, 9, 4, HG], F32), ("cc", [P, CT, 29], F32)])
        hcol, rhsx = small[0:SH, 0:8], small[0:SH, 8:17]
        sq = [at(f"sq{i}", [P, T], off=T0 + i * T * 4) for i in range(2)]
        rs = at("rs", [P, T], off=T0 + 2 * T * 4)
        xs = at("xs", [P, XT, T], off=X1)
        zs = at("zs", [P, XT, T], off=X1 + XT * T * 4)
        yH = at("yH", [P, XT, T], F32R, off=R1)
        yL = at("yL", [P, XT, T], F32R, off=R1 + XT * T * 4)
        (bc,), o = region(R1, "ssd", [("bc", [P, 2, T], F32)])
        (craw0, craw1, cacc), _ = region(o, "ssd", [(f"c{i}", [P, CWID], F32) for i in range(3)])
        craw = [craw0, craw1]
        conv_end, scan0 = o + 3 * CWID * 4, o
        (s00, s01, e1, bcb, xe, e0, xtok, ytok, st), o = region(o, "ssd", [
            ("s00", [P, DB, P], F32), ("s01", [P, DB, P], F32), ("e1", [P, HG, P], F32), ("bcb", [P, 256], F32),
            ("xe", [P, 512], F32), ("e0", [P, HG, P], F32), ("xtok", [P, 512], F32), ("ytok", [P, 512], F32),
            ("st", [P, 512], F32)])
        assert scan0 + 3 * 4096 + 1024 + 2048 >= conv_end
        assert o <= X0
        dec = [e0, e1]
        cm = at("cm", [P, DB * 72], off=T0 + 4096)
        bm = at("bm", [NS, DB, P], off=scan0 + 2 * 4096)
        (cr0, cr1, s0t), _ = region(T0, "ssd", [("cr0", [P, HG, P], F32), ("cr1", [P, HG, P], F32), ("s0t", [P, DB, P], F32)])
        cumrow = [cr0, cr1]
        s0 = [s00, s01]

        qkv = [[at(f"qkv{gr}{k}", [P, SEQ], off=X1 + (3 * gr + k) * SEQ * 4) for k in range(3)] for gr in range(NG)]
        qkvs = at("qkvs", [P, 3, NG, NJ, NS], off=X1 + 9 * SEQ * 4)
        (ob0, ob1, ob2, vt0, vt1, vt2, kt0, kt1, kt2), o = region(R1, "at", [(f"o{i}", [P, NT, 132], F32) for i in range(3)] + [
            (f"v{i}", [P, NT, P], F32) for i in range(3)] + [("k0", [P, 1, P], F32), ("k1", [P, 4, P], F32), ("k2", [P, NT, P], F32)])
        assert o <= X0
        obuf, vtok, ktok = [ob0, ob1, ob2], [vt0, vt1, vt2], [kt0, kt1, kt2]
        (sb0, sb1, pt0, pt1, mask01, mask2, mk8), o = region(X0, "at", [
            ("s0", [P, 2, 256], F32), ("s1", [P, 2, 256], F32), ("p0", [P, 4, P], F32), ("p1", [P, 4, P], F32),
            ("mask01", [P, 256], F32), ("mask2", [P, P], F32), ("mk8", [DS, 1176], F32)])
        sbuf, pt = [sb0, sb1], [pt0, pt1]
        mb = [at(f"mb{i}", [P, NT, NG, 132], off=X1 + i * NT * NG * 132 * 4) for i in range(2)]
        (mmin, marg, mwd, mden), _ = region(X1 + 2 * NT * NG * 132 * 4, "mg", [
            ("min", [P, NT, 2], F32), ("arg", [P, NT, NG, 2], F32), ("wd", [P, NT, NG, 2], F32), ("den", [P, NT, 2], F32)])
        aH, aL = yH, yL
        (kraw, ktr0, ktr1, sS, vnew), o = region(X0, "sm", [
            ("kraw", [P, 9, 512], F32), ("kt0", [P, 1152], F32), ("kt1", [P, 1152], F32), ("s", [NS, 1176], F32), ("vn", [24, 512], F32)])
        assert o <= X1
        ktr = [ktr0, ktr1]
        (vraw, maskS, pts, qblk, kvn, aS), o = region(X1, "sm", [
            ("vraw", [P, 9, 512], F32), ("mask", [NS, 1176], F32), ("pt", [P, 10, NS], F32), ("qb", [P, NG, NJ, NS], F32),
            ("kvn", [NS, 2, 512], F32), ("aS", [P, NJ, NS], F32)])
        goff = (o, o + TH[0][1] * 4, X1 + 9 * SEQ * 4 + 9 * NJ * NS * 4)
        gpart = [at(f"gpart{c}", [P, TH[0][1]], off=goff[c]) for c in range(3)]
        assert goff[1] + TH[0][1] * 4 <= X1 + 9 * SEQ * 4 and goff[2] + TH[0][1] * 4 <= T0 + 3 * T * 4
        nm3, sden = small[0:NS, 80:84], small[0:NS, 84:86]
        gates = [at("gate_a", [P, KD, T], off=H0), at("gate_b", [P, KD, T], off=H0 + KD * T * 4)]
        m2 = at("m2", [P, KD, T], off=R1)
        x1 = at("x1", [P, KD, T], off=X1)
        uH = [at(f"uH{i}", [P, 2, T], F32R, off=X0 + i * 4 * T * 4) for i in range(2)]
        uL = [at(f"uL{i}", [P, 2, T], F32R, off=X0 + i * 4 * T * 4 + 2 * T * 4) for i in range(2)]
        (yo0, yo1, ncb, ncrow), o = region(X0, "fin", [
            ("y0", [P, D], F32), ("y1", [P, D], F32), ("ncb", [P, CT, 27], F32), ("ncrow", [27, CONVD], F32)])
        yo = [yo0, yo1]

        ps = [ctx.enter_context(nc.psum_tensor(f"ps{i}", [P, 512], F32)) for i in range(8)]
        G, A = ps[0:3], ps[3:8]

        raw_in = [sem(f"raw_in{i}") for i in range(RAW)]
        w_hi, w_split = sem("w_hi"), sem("w_split")
        g_ready = [sem(f"g_ready{c}") for c in range(3)]
        g_free = [sem(f"g_free{c}") for c in range(3)]
        x_in, par_in, col_in, consts, selfill = sem("x_in"), sem("par_in"), sem("col_in"), sem("consts"), sem("selfill")
        par_ps, par_out, xt_ps, xt_act, xt_dve = sem("par_ps"), sem("par_out"), sem("xt_ps"), sem("xt_act"), sem("xt_dve")
        sq_ready, sq_used, rs_ready = sem("sq_ready"), sem("sq_used"), sem("rs_ready")
        hv_ready, hH_ready, hL_ready = sem("hv_ready"), sem("hH_ready"), sem("hL_ready")
        scr_out = sem("scr_out")
        dt_act, dt_dve, dt_ps, dt_scr = sem("dt_act"), sem("dt_dve"), sem("dt_ps"), sem("dt_scr")
        pause = sem("pause")

        def gap(c, rows=P):
            return G[c][0:rows, 0:TH[c][1] - TH[c][0]]

        def cols(a, c):
            return a[:, TH[c][0]:TH[c][1]]

        def hv(k, c):
            w = TH[c][1] - TH[c][0]
            o = (k % 2) * TH[0][1]
            return sq[k % 4 // 2][:, o:o + w]

        def alone(eng):
            eng.sem_inc(pause, 1)

        amask, copies, mk_out, att_out = sem("amask"), sem("copies"), sem("mk_out"), sem("att_out")
        vt_ready, vt_out, s_ready, s_min, p_done = sem("vt_ready"), sem("vt_out"), sem("s_ready"), sem("s_min"), sem("p_done")
        pt_ready, pt_out, pv_ready, ob_out = sem("pt_ready"), sem("pt_out"), sem("pv_ready"), sem("ob_out")
        unit_out = [sem(f"unit_out{i}") for i in range(NG)]
        mb_in = [sem("mb_in0"), sem("mb_in1")]
        mg, mg_exp, mo_ready, mt_ready, aH_ready, aL_ready = sem("mg"), sem("mg_exp"), sem("mo_ready"), sem("mt_ready"), sem("aH_ready"), sem("aL_ready")
        kvn_ps, kvn_ev, kvn_out, mS_in = sem("kvn_ps"), sem("kvn_ev"), sem("kvn_out"), sem("mS_in")
        k_in, v_in, qb_ready, k_fill, kt_dve, kt_act, sc_done = (sem("k_in"), sem("v_in"), sem("qb_ready"), sem("k_fill"),
                                                                sem("kt_dve"), sem("kt_act"), sem("sc_done"))
        sm_dve, sm_exp, sp_ready, spt_dve, spt_act, spv_ready, aS_out = (sem("sm_dve"), sem("sm_exp"), sem("sp_ready"), sem("spt_dve"),
                                                                        sem("spt_act"), sem("spv_ready"), sem("aS_out"))
        ba_in, xt_in, x1_done, facc_zero = sem("ba_in"), sem("xt_in"), sem("x1_done"), sem("facc_zero")
        v_done, uH_ready, uL_ready, add_done = sem("v_done"), sem("uH_ready"), sem("uL_ready"), sem("add_done")
        y_done, yt_ready, yo_dve, yo_act, y_out, ncb_in, nct_ready, nct_out = (sem("y_done"), sem("yt_ready"), sem("yo_dve"), sem("yo_act"),
                                                                              [sem("y_out0"), sem("y_out1")], sem("ncb_in"), sem("nct_ready"), sem("nct_out"))

        def tokens(a, gr, i):
            if gr == 0:
                return a[:, i * P:(i + 1) * P]
            if gr == 1:
                return a[:, 512 * (i // 4) + i % 4:512 * (i // 4 + 1):4]
            return a[:, i * P:(i + 1) * P]

        def keys(a, gr, i):
            if gr == 0 and i:
                return a[:, (i - 1) * P:(i + 1) * P]
            if gr == 1 and i >= 4:
                return a.rearrange("p (n a r) -> p r n a", n=2, r=4)[:, i % 4, :, :]
            return tokens(a, gr, i)

        def blocks(gr, i):
            if gr == 0 and i:
                return [i - 1, i]
            if gr == 1 and i >= 4:
                return [i - 4, i]
            return [i]

        def k_tile(gr, i):
            return {0: i - 7, 1: i - 4, 2: i}[gr] if i >= (7, 4, 0)[gr] else None

        mix_in = [sem(f"mix_in{m}") for m in range(KD)]
        gate_out = [sem(f"gate_out{c}") for c in range(3)]
        mix_step, nct_ev = sem("mix_step"), sem("nct_ev")
        pad_ready, conv_act, conv_dve, conv_done = sem("pad_ready"), sem("conv_act"), sem("conv_dve"), sem("conv_done")
        cc_in, tok_in, nc_out = sem("cc_in"), sem("tok_in"), sem("nc_out")
        cr_in = [sem("cr_in0"), sem("cr_in1")]
        grp = sem("grp")
        a_ready, a_copied, seg_done, exp_done = sem("a_ready"), sem("a_copied"), sem("seg_done"), sem("exp_done")
        el_done, w_done, xe_done, b_ready, d_step = sem("el_done"), sem("w_done"), sem("xe_done"), sem("b_ready"), sem("d_step")
        y_ready, yev_done, cmbm = sem("y_ready"), sem("yev_done"), sem("cmbm")
        s0_in = [sem("s0_in0"), sem("s0_in1")]
        s0_tr, s0t_dve, s0t_act, s0_up, s0_new, ssm_out = sem("s0_tr"), sem("s0t_dve"), sem("s0t_act"), sem("s0_up"), sem("s0_new"), sem("ssm_out")
        st_ready, st_ev, st_out = sem("st_ready"), sem("st_ev"), sem("st_out")
        zs_silu, gate_done, yn_done, yH_ready, yL_ready = sem("zs_silu"), sem("gate_done"), sem("yn_done"), sem("yH_ready"), sem("yL_ready")
        acc_zero, acc_add, ba_out = sem("acc_zero"), sem("acc_add"), sem("ba_out")

        ZG = [(m, c) for m in range(XT) for c in range(3)]
        NCH = NT + 1
        DSTEPS = [2] + [4] * 7 + [2]
        DSUM = sum(DSTEPS)

        def chunk(c):
            return (c * P, P) if c < NT else (SEQ, NS)

        win = w_in[0].rearrange("(k p) n -> p k n", p=P)
        wao = w_attn_out[0].rearrange("(k p) n -> p k n", p=P)
        wou = w_out[0].rearrange("(k p) n -> p k n", p=P)
        wup = w_up[0].rearrange("(k p) n -> p k n", p=P)

        def ssd_chunks(g):
            firsts = [XBC0 + DI + g * NST, XBC0 + DI + SG * NST + g * NST]
            firsts += [XBC0 + g * XT * P + m * P for m in range(XT)]
            firsts += [Z0 + g * XT * P + m * P for m in range(XT)]
            return [(win[:, :, ds(f, P)], KD, P) for f in firsts] + [
                (wssd_rows(g)[:, :, m * P:(m + 1) * P], XT, P) for m in range(KD)]

        def wssd_rows(g):
            return w_ssd_out[0, ds(g * XT * P, XT * P), :].rearrange("(k p) n -> p k n", p=P)

        def att_chunks(j):
            return [(win[:, :, ds(gr * 3 * AW + kind * AW + j * P, P)], KD, P) for gr in range(NG) for kind in range(3)]

        def gate_chunk(m, k):
            return win[:, :, ds(GATE0 + k * D + m * P, P)], KD, P

        def up_chunks(k):
            return [(wup[:, :, ds(o + (2 * k + i) * P, P)], KD, P) for i in range(2) for o in (0, FF)]

        def down_chunks(k):
            rows = w_down[0, ds(k * 2 * P, 2 * P), :].rearrange("(k p) n -> p k n", p=P)
            return [(rows[:, :, 0:512], 2, 512), (rows[:, :, 512:1024], 2, 512)]

        def stages():
            yield C_DT, 1, lambda i: [(win[:, :, DT0:DT0 + SH], KD, SH)]
            yield C_SSD, SG, ssd_chunks
            yield C_ATT, NJ // 2, lambda i: att_chunks(2 * i) + att_chunks(2 * i + 1)
            yield C_OUT, 1, lambda i: [(wou[:, :, m * P:(m + 1) * P], KD, P) for m in range(KD)]
            yield C_FF, 1, lambda i: up_chunks(0)
            yield C_FF + 4, 5, lambda i: (up_chunks(2 * i + 1) + down_chunks(2 * i)
                                          + up_chunks(2 * i + 2) + down_chunks(2 * i + 1))
            yield C_FF + 4 + 60, 1, lambda i: down_chunks(FT // 2 - 1)

        block = ctx.enter_context(nc.Block())

        @block.sync
        def _(sp):
            sp.dma_start(rows48[0:8, :], pre_mix_norm[0].rearrange("(k p) -> k p", p=P)).then_inc(par_in, 16)
            sp.dma_start(rows48[8:16, :], post_mix_norm[0].rearrange("(k p) -> k p", p=P)).then_inc(par_in, 16)
            sp.dma_start(rows48[16:24, :], pre_ffn_norm[0].rearrange("(k p) -> k p", p=P)).then_inc(par_in, 16)
            sp.dma_start(rows48[24:32, :], post_ffn_norm[0].rearrange("(k p) -> k p", p=P)).then_inc(par_in, 16)
            sp.dma_start(rows48[32:48, :], ssd_norm[0].rearrange("(k p) -> k p", p=P)).then_inc(par_in, 16)
            sp.dma_start(convrows[0:4, :], conv_w[0]).then_inc(par_in, 16)
            sp.dma_start(convrows[4:5, :], conv_b).then_inc(par_in, 16)
            sp.dma_start(strows[:, :], state_conv[0].rearrange("b i n -> (b i) n")).then_inc(par_in, 16)
            sp.dma_start(xin[:, :, :], x_prompt[0].rearrange("(i p) d -> p i d", p=P)).then_inc(x_in, 16)
            sp.dma_start(xins[:, :], x_sample.rearrange("b s d -> (b s) d")).then_inc(x_in, 16)
            sp.dma_start(hcol[:, 0:1], dt_bias.rearrange("a h -> h a")).then_inc(col_in, 16)
            sp.dma_start(hcol[:, 1:2], a_log.rearrange("a h -> h a")).then_inc(col_in, 16)
            sp.dma_start(rhsx[:, 8:9], d_skip.rearrange("a h -> h a")).then_inc(col_in, 16)

            def load(n, src, kt, w, seq):
                if seq >= RAW - 1:
                    sp.wait_ge(w_split, n - RAW + 2)
                    if not isinstance(n, int):
                        alone(sp)
                sp.dma_start(wraw[seq % RAW][:, 0:kt * w].rearrange("p (k n) -> p k n", k=kt), src)\
                    .then_inc(raw_in[seq % RAW], 16)

            for s in unit_out:
                sp.sem_inc(s, 1)

            def send_unit(j, gr):
                n = j * NG + gr
                sp.wait_ge(ob_out, NT * (n + 1) + 2)
                sp.wait_ge(vt_out, NT * (n + 1) + 2)
                pair = slice(2 * j, 2 * j + 2)

                def send(dst, src):
                    sp.dma_start(dst, src).then_inc(unit_out[gr], 16)

                def heads_of(kv, rows):
                    return kvp[gr][0, 0, rows, kv, pair, :].rearrange("t h e -> t (h e)")

                if gr == 0:
                    send(o_scr[j, 0].rearrange("(i p) n -> p i n", p=P), obuf[0][:, :, :])
                    send(heads_of(0, slice(0, P)), ktok[0][:, 0, :])
                    send(heads_of(1, slice(0, P)), vtok[0][:, NT - 1, :])
                elif gr == 1:
                    for n in range(2):
                        send(o_scr[j, 1, 512 * n:512 * n + 512].rearrange("(a r) c -> a r c", r=4), obuf[1][:, 4 * n:4 * n + 4, :])
                    send(heads_of(0, slice(0, 512)).rearrange("(a r) c -> a r c", r=4), ktok[1][:, :, :])
                    send(heads_of(1, slice(0, 512)).rearrange("(a r) c -> a r c", r=4), vtok[1][:, 4:8, :])
                else:
                    for r in range(2):
                        q = slice(64 * r, 64 * r + 64)
                        send(o_scr[j, 2].rearrange("(a i r) c -> r a i c", i=NT, r=2)[r], obuf[2][q, :, :])
                        send(heads_of(0, slice(0, SEQ)).rearrange("(a i r) c -> r a i c", i=NT, r=2)[r], ktok[2][q, :, :])
                        send(heads_of(1, slice(0, SEQ)).rearrange("(a i r) c -> r a i c", i=NT, r=2)[r], vtok[2][q, :, :])

            def copy_rows(gr, b, n):
                sp.dma_start(kvs[gr][0, b:b + n, 0:ROWS[gr] - DS].rearrange("b r k h e -> b r (k h e)"),
                             caches[gr][0, b:b + n, DS:ROWS[gr]].rearrange("b r k h e -> b r (k h e)")).then_inc(copies, 16)

            def merge_load(j):
                sp.wait_ge(unit_out[0], 16 * 3 * (j + 1) + 1)
                sp.wait_ge(unit_out[1], 16 * 4 * (j + 1) + 1)
                sp.wait_ge(unit_out[2], 16 * 6 * (j + 1) + 1)
                if j == 0:
                    sp.wait_ge(pv_ready, NG * NJ * NT)
                if j >= 2:
                    sp.wait_ge(mt_ready, j - 1)
                for gr in range(NG):
                    sp.dma_start(mb[j % 2][:, :, gr, :], o_scr[j, gr].rearrange("(i p) n -> p i n", p=P)).then_inc(mb_in[j % 2], 16)

            def load_k(b):
                sp.dma_start(kraw[:, 0, :], caches[0][0, ds(b, 1), :, 0].rearrange("b r h e -> (b r) (h e)")).then_inc(k_in, 16)
                load_rest(kraw, b, 0, k_in)

            def load_v(b):
                sp.dma_start(vraw[:, 0, :], caches[0][0, ds(b, 1), :, 1].rearrange("b r h e -> (b r) (h e)")).then_inc(v_in, 16)
                load_rest(vraw, b, 1, v_in)
                for gr in range(NG):
                    sp.dma_start(vnew[DS * gr:DS * gr + DS, :],
                                 kvs[gr][0, ds(b, 1), ROWS[gr] - DS:ROWS[gr], 1].rearrange("b r h e -> (b r) (h e)")).then_inc(v_in, 16)

            def load_rest(dst, b, kv, s):
                sp.dma_start(dst[:, 1:5, :], caches[1][0, ds(b, 1), :, kv].rearrange("b (t p) h e -> p (b t) (h e)", p=P)).then_inc(s, 16)
                for t in range(4):
                    rows = caches[2][0, ds(b, 1), 256 * t:256 * t + 256, kv].rearrange("b (a i) h e -> (b a) i (h e)", i=16)
                    sp.dma_start(dst[:, 5 + t, :], rows[:, 0:DS, :]).then_inc(s, 16)

            for stage, (first, rounds, chunks) in enumerate(stages()):
                per = len(chunks(0))
                if stage == 2:
                    for w in range(NG * NJ):
                        for k, (src, kt, wd) in enumerate(att_chunks(w // NG)[3 * (w % NG):3 * (w % NG) + 3]):
                            load(first + 3 * w + k, src, kt, wd, first + 3 * w + k)
                            if k == 2:
                                if w < DB:
                                    copy_rows(2, w, 1)
                                else:
                                    copy_rows(1, 2 * (w - DB), 2)
                                    copy_rows(0, 2 * (w - DB), 2)
                            if k == 1 and w >= 2:
                                send_unit((w - 2) // NG, (w - 2) % NG)
                            if k == 1 and w == 2:
                                sp.wait_ge(amask, 3)
                                sp.dma_start(mk_scr, mk8[:, :]).then_inc(mk_out, 16)
                    for k in range(2):
                        load(C_GATE + k, *gate_chunk(0, k), C_GATE + k)
                    send_unit(NJ - 1, 1)
                    send_unit(NJ - 1, 2)
                    sp.wait_ge(mk_out, 16)
                    for j in range(2):
                        merge_load(j)
                    load_k(0)
                    for k in range(2):
                        load(C_GATE + 2 + k, *gate_chunk(1, k), C_GATE + 2 + k)
                    for j in range(2, NJ):
                        merge_load(j)
                    for gr in range(NG):
                        sp.wait_ge(kvn_ev, 2 * gr + 2)
                        for kv in range(2):
                            sp.dma_start(kvs[gr][0, :, ROWS[gr] - DS:ROWS[gr], kv].rearrange("b i h e -> b i (h e)"),
                                         kvn[:, kv, :]).then_inc(kvn_out, 16)
                    sp.wait_ge(mt_ready, NJ)
                    sp.dma_start(maskS[:, :], mk_scr.unsqueeze(0).to_broadcast([HEADS, DS, 1176])).then_inc(mS_in, 16)
                    sp.wait_ge(kvn_out, 16 * 6)
                    load_v(0)
                    sp.wait_ge(k_fill, 12)
                    load_k(1)
                    with sp.Fori(0, DB - 2) as b:
                        for k in range(2):
                            load(b * 2 + (C_GATE + 4 + k), *gate_chunk(b + 2, k), C_GATE + 4 + k)
                        sp.wait_ge(k_fill, b * 12 + 24)
                        alone(sp)
                        load_k(b + 2)
                        sp.wait_ge(spv_ready, b + 1)
                        alone(sp)
                        load_v(b + 1)
                    for m in range(2):
                        load(C_PROJ + m, wao[:, :, m * P:(m + 1) * P], NJ, P, C_PROJ + m)
                    sp.wait_ge(spv_ready, DB - 1)
                    load_v(DB - 1)
                    for q in gate_out:
                        sp.wait_ge(q, 32 * KD + 1)
                    sp.wait_ge(g_ready[2], U_PROJ - 1)
                    for m in range(2):
                        for k in range(2):
                            sp.dma_start(gates[k][:, m, :], gate_scr[k, m]).then_inc(mix_in[m], 16)
                    sp.wait_ge(spv_ready, DB)
                    for m in range(KD):
                        if m >= 2:
                            for k in range(2):
                                sp.dma_start(gates[k][:, m, :], gate_scr[k, m]).then_inc(mix_in[m], 16)
                        sp.dma_start(acc8[:, m, :], ba_scr[:, m, :]).then_inc(mix_in[m], 16)
                        if m + 2 < KD:
                            load(C_PROJ + m + 2, wao[:, :, (m + 2) * P:(m + 3) * P], NJ, P, C_PROJ + m + 2)
                    continue
                if stage == 3:
                    sp.wait_ge(aL_ready, 2 * NJ + 1)
                    sp.dma_start(x1[:, :, :], xt_scr).then_inc(xt_in, 16)
                if rounds == 1:
                    for k, (src, kt, w) in enumerate(chunks(0)):
                        load(first + k, src, kt, w, first + k)
                    continue
                with sp.Fori(0, rounds) as i:
                    for k, (src, kt, w) in enumerate(chunks(i)):
                        load(i * per + (first + k), src, kt, w, first + k)
                        if stage == 1 and k == 3:
                            sp.wait_ge(dt_scr, 16 * 3)
                            sp.wait_ge(yL_ready, i * 3 * XT + 1)
                            alone(sp)
                            sp.dma_start(tokg[:, :, :, :].rearrange("p a b c -> p (a b c)"),
                                         tok_scr[:, ds(i, 1), :].rearrange("p a n -> p (a n)")).then_inc(tok_in, 16)
                            sp.dma_start(ccg[:, 0, :], cc_scr[:, ds(i + 16, 1), :].rearrange("p a n -> p (a n)")).then_inc(cc_in, 16)
                            sp.dma_start(ccg[:, 1, :], cc_scr[:, ds(i + 20, 1), :].rearrange("p a n -> p (a n)")).then_inc(cc_in, 16)
                            sp.dma_start(ccg[:, 2:6, :], cc_scr[:, ds(i * 4, 4), :]).then_inc(cc_in, 16)
            for c in range(3):
                sp.wait_ge(g_ready[c], U_FF + (FT // 2) * FF_USES)
            sp.dma_start(ncb[:, :, :], nc_scr.rearrange("t p n -> p t n")).then_inc(ncb_in, 16)
            sp.wait_ge(copies, 16 * (DB + 2 * (NG * NJ - DB)))
            sp.wait_ge(ssm_out, 16 * 16)
            sp.wait_ge(st_out, 16 * SG)
            sp.wait_ge(nct_out, 16 * 2)
            sp.wait_ge(y_out[0], 16 * 5)
            sp.wait_ge(y_out[1], 16 * 4)

        @block.gpsimd
        def _(pool):
            pool.sem_inc(w_split, 1)
            pool.memset(ident[:, :], 0.0).then_inc(selfill, 1)
            pool.memset(ones[:, :], 1.0).then_inc(selfill, 1)
            pool.memset(smask[:, :], 0.0).then_inc(selfill, 1)
            pool.memset(smaskS[:, :], 0.0).then_inc(selfill, 1)
            pool.memset(bmask[:, :], 1.0).then_inc(selfill, 1)
            pool.memset(eps[:, :], EPS).then_inc(selfill, 1)
            pool.wait_ge(selfill, 6)
            pool.affine_select(out=ident[:, :], in_=ident[:, :], compare_op=ALU.not_equal, fill=1.0, base=0,
                               pattern=[[-1, P]], channel_multiplier=1).then_inc(consts, 1)
            pool.affine_select(out=smask[:, :], in_=smask[:, :], compare_op=ALU.is_ge, fill=NEG, base=0,
                               pattern=[[1, P]], channel_multiplier=-1).then_inc(consts, 1)
            pool.affine_select(out=smaskS[:, :], in_=smaskS[:, :], compare_op=ALU.is_ge, fill=NEG, base=0,
                               pattern=[[1, NS]], channel_multiplier=-1).then_inc(selfill, 1)
            pool.wait_ge(selfill, 7)
            pool.affine_select(out=smaskS[:, :], in_=smaskS[:, :], compare_op=ALU.is_ge, fill=NEG, base=0,
                               pattern=[[-DS, DB], [0, DS]], channel_multiplier=1).then_inc(consts, 1)
            pool.affine_select(out=bmask[:, :], in_=bmask[:, :], compare_op=ALU.is_ge, fill=0.0, base=0,
                               pattern=[[-DS, DB]], channel_multiplier=1).then_inc(selfill, 1)
            pool.wait_ge(selfill, 8)
            pool.affine_select(out=bmask[:, :], in_=bmask[:, :], compare_op=ALU.is_ge, fill=0.0, base=DS - 1,
                               pattern=[[DS, DB]], channel_multiplier=-1).then_inc(consts, 1)

            def split(n, u, kt, w, seq, guard=True):
                a, b, k = wraw[seq % RAW], seq % SPL, kt * w
                pool.wait_ge(raw_in[seq % RAW], raw_count(n, seq))
                if guard:
                    pool.wait_ge(g_ready[2], u)
                alone(pool)
                pool.tensor_copy(wH[b][:, 0:k], a[:, 0:k]).then_inc(w_hi, 1)
                pool.wait_ge(w_hi, n + 1)
                pool.tensor_tensor(wL[b][:, 0:k], a[:, 0:k], wH[b][:, 0:k].bitcast(F32), ALU.subtract).then_inc(w_split, 1)

            def raw_count(n, seq):
                if isinstance(n, int):
                    return 16 * (n // RAW + 1)
                return n * 8 + (16 - 8 * (seq % RAW))

            split(0, 0, KD, SH, 0, guard=False)
            pool.wait_ge(xt_ps, KD)
            pool.memset(dtsel[:, :, :], 0.0).then_inc(selfill, 1)
            pool.wait_ge(selfill, 9)
            pool.affine_select(out=dtsel[:, :, :].rearrange("h a (b c) -> h (a b) c", c=64),
                               in_=dtsel[:, :, :].rearrange("h a (b c) -> h (a b) c", c=64),
                               compare_op=ALU.not_equal, fill=1.0, base=0, pattern=[[-1, SH], [0, 64]],
                               channel_multiplier=1).then_inc(consts, 1)
            split(1, 0, KD, P, 1, guard=False)
            split(2, 0, KD, P, 2, guard=False)
            pool.wait_ge(hL_ready, 3 * KD)
            pool.wait_ge(scr_out, 16)
            pool.memset(acc8[:, :, :], 0.0).then_inc(acc_zero, 1)

            def spread_xe(g, c):
                o, n = chunk(c)
                pool.wait_ge(a_copied, g * 2 * NCH + 2 * (c + 1))
                pool.tensor_tensor(xe[0:n, :].rearrange("p (h e) -> p h e", e=64),
                                   xtok[0:n, :].rearrange("p (h e) -> p h e", e=64),
                                   tokg[0:n, c, 2, :].unsqueeze(2).to_broadcast([n, HG, 64]), ALU.mult).then_inc(xe_done, 1)

            def used(k, g):
                return g * SSD_USES + (U_SSD + k + 1 + (1 if k >= 2 + 2 * XT else 0))

            with pool.Fori(0, SG) as g:
                for k in range(SSD_CH):
                    kt = KD if k < 2 + 2 * XT else XT
                    n = C_SSD + k
                    if k == 9:
                        for c in range(3):
                            spread_xe(g, c)
                    if k == 10:
                        for c in range(3, 6):
                            spread_xe(g, c)
                    if k == 11:
                        for c in range(6, 9):
                            spread_xe(g, c)
                    if k == 0 or k == 1:
                        continue
                    split(g * SSD_CH + n, used(k - SPL, g) if k >= SPL else g * SSD_USES + U_SSD, kt, P, n)
                for k in range(2):
                    n = C_SSD + SSD_CH + k
                    split(g * SSD_CH + n, used(SSD_CH + k - SPL, g), KD, P, n)
            filled = [9]

            def fill(ins):
                filled[0] += 1
                ins.then_inc(selfill, 1)
                pool.wait_ge(selfill, filled[0])

            def keep(a, op, other, offset, pattern, cm):
                return pool.affine_select(out=a, in_=a, compare_op=op, fill=other, base=offset, pattern=pattern, channel_multiplier=cm)

            split(C_ATT + 2, U_ATT, KD, P, C_ATT + 2)
            pool.wait_ge(ba_out, 16)
            fill(pool.memset(mask01[:, :], 0.0))
            fill(keep(mask01[:, :], ALU.is_ge, NEG, 0, [[1, 256]], -1))
            keep(mask01[:, :], ALU.is_ge, NEG, P, [[-1, 256]], 1).then_inc(amask, 1)
            fill(pool.memset(mask2[:, :], 0.0))
            fill(keep(mask2[:, :], ALU.is_ge, NEG, 0, [[-1, P]], 1))
            keep(mask2[:, :], ALU.is_ge, NEG, 63, [[64, 2], [0, 64]], -1).then_inc(amask, 1)
            fill(pool.memset(mk8[:, :], NEG))
            fill(pool.memset(mk8[:, 0:136], 0.0))
            fill(keep(mk8[:, 0:P], ALU.is_ge, NEG, 0, [[1, P]], -1))
            fill(keep(mk8[:, 128:136], ALU.is_ge, NEG, 0, [[-1, DS]], 1))
            for off in (0, 4):
                fill(keep(mk8[:, 136:144], ALU.not_equal, 0.0, off, [[1, DS]], -1))
                fill(keep(mk8[:, 152:664], ALU.not_equal, 0.0, off, [[0, P], [1, 4]], -1))
            fill(keep(mk8[:, 144:152], ALU.not_equal, 0.0, 0, [[1, DS]], -1))
            fill(keep(mk8[:, 152:664], ALU.is_ge, NEG, 0, [[1, 512]], -1))
            keep(mk8[:, 664:1176], ALU.not_equal, 0.0, 0, [[0, 64], [1, DS]], -1).then_inc(amask, 1)

            with pool.Fori(0, 5) as i:
                for t in range(6):
                    split(i * 6 + (C_ATT + 3 + t), i * 6 + (U_ATT + 1 + t), KD, P, C_ATT + 3 + t)
            for k in range(33, 36):
                split(C_ATT + k, U_ATT + k - 2, KD, P, C_ATT + k)
            for k in range(2):
                split(C_GATE + k, U_SAM - 2 + k, KD, P, C_GATE + k)
            pool.wait_ge(mt_ready, NJ)
            fill(pool.memset(qblk[:, :, :, :], 0.0))

            def queries(b):
                pool.wait_ge(w_split, b * 2 + (C_GATE + 3))
                pool.wait_ge(sc_done, b * NJ + 1)
                alone(pool)
                for j in range(NJ):
                    for s in range(2):
                        ins = pool.tensor_copy(qblk[64 * s:64 * s + 64, :, j, (2 * j + s) * DS:(2 * j + s + 1) * DS],
                                               qkvs[64 * s:64 * s + 64, 0, :, j, ds(b * DS, DS)])
                ins.then_inc(qb_ready, 1)
                pool.wait_ge(qb_ready, b + 1)

            with pool.Fori(0, DB - 1) as b:
                queries(b)
                for k in range(2):
                    split(b * 2 + (C_GATE + 2 + k), b * 3 + (U_SAM + 1 + k), KD, P, C_GATE + k)
            queries(DB - 1)
            for m in range(KD):
                split(C_PROJ + m, U_PROJ + max(m - 2, -1), NJ, P, C_PROJ + m)
            for m in range(KD):
                split(C_OUT + m, U_OUT + m - 2, KD, P, C_OUT + m)
            for t in range(3):
                split(C_FF + t, U_OUT + 6 + t, KD, P, C_FF + t)
            pool.wait_ge(x1_done, 2 * KD)
            pool.memset(m2[:, :, :], 0.0).then_inc(facc_zero, 1)
            split(C_FF + 3, U_FF + 1, KD, P, C_FF + 3)
            ends = (1, 2, 3, 4, 8, 12, 13, 14, 15, 16, 20, 24)
            with pool.Fori(0, 5) as i:
                for t in range(12):
                    kt, w = (2, 512) if t % 6 >= 4 else (KD, P)
                    u = ends[t - 3] if t >= 3 else t - 2
                    split(i * 12 + (C_FF + 4 + t), i * 24 + (U_FF + 4 + u), kt, w, C_FF + 4 + t)
            for t in range(2):
                split(C_FF + 64 + t, U_FF + 124 - 8 + 4 * t, 2, 512, C_FF + 64 + t)
        @block.scalar
        def _(act):
            def evac(c, u, pieces):
                act.wait_ge(g_ready[c], u)
                for k, (dst, src) in enumerate(pieces):
                    ins = act.copy(dst, src)
                ins.then_inc(g_free[c], 1)

            def squares(src, n, base, used, before=None):
                for f in range(n):
                    if before:
                        before(f)
                    if f >= 2:
                        act.wait_ge(sq_used, used + f - 1)
                    act.activation(sq[f % 2][:, :], src[:, f, :], ACT.Square).then_inc(sq_ready, 1)

            def roots(n, u):
                for c in range(3):
                    act.wait_ge(g_ready[c], u)
                    act.activation(cols(rs, c), gap(c), ACT.Sqrt, bias=eps[:, 0:1], scale=1.0 / (n * P))\
                       .then_inc(g_free[c], 1)

            def halves(base):
                k = 0
                for c in range(3):
                    for f in range(KD):
                        act.wait_ge(hv_ready, base + k + 1)
                        act.copy(cols(hH[:, f, :], c), hv(k, c)).then_inc(hH_ready, 1)
                        k += 1

            for f in range(KD):
                act.wait_ge(xt_ps, f + 1)
                bank = A[0] if f % 2 == 0 else A[3]
                act.copy(acc8[:, f, 0:512], bank[:, :]).then_inc(xt_act, 1)
            act.wait_ge(xt_act, KD)
            act.wait_ge(xt_dve, KD)
            act.dma_start(xt_scr, acc8[:, :, :]).then_inc(scr_out, 16)
            squares(acc8, KD, 0, 0)
            roots(KD, U_NORM0)
            act.wait_ge(par_out, 4)
            act.dma_start(cc_scr, ccd[:, :, :]).then_inc(dt_scr, 16)
            halves(0)

            act.wait_ge(col_in, 48)
            for c in range(3):
                act.wait_ge(g_ready[c], U_DT)
                ins = act.activation(cols(dv, c), gap(c, SH), ACT.Identity, bias=hcol[:, 0:1], scale=1.0)
                ins.then_inc(g_free[c], 1)
            act.wait_ge(g_free[2], U_DT)
            act.activation(de[:, :], dv[:, :], ACT.Abs).then_inc(dt_act, 1)
            act.wait_ge(dt_act, 1)
            act.activation(de[:, :], de[:, :], ACT.Exp, scale=-1.0).then_inc(dt_act, 1)
            act.activation(hcol[:, 2:3], hcol[:, 1:2], ACT.Exp).then_inc(dt_act, 1)
            act.wait_ge(dt_dve, 1)
            act.activation(dl[:, :], du[:, :], ACT.Ln).then_inc(dt_act, 1)
            act.wait_ge(dt_dve, 16)
            act.dma_start(cum_scr, dcum[:, :]).then_inc(dt_scr, 16)
            act.activation(de[:, :], de[:, :], ACT.Exp).then_inc(dt_act, 1)
            act.activation(dl[:, :], dcum[:, :], ACT.Exp).then_inc(dt_act, 1)
            act.wait_ge(dt_ps, 1)
            act.activation(ecl[:, :, :], A[3][:, 0:144].rearrange("p (a b) -> p a b", b=9)[:, :, 0:8], ACT.Exp).then_inc(dt_act, 1)
            act.copy(dsk[:, :], A[3][:, 0:144].rearrange("p (a b) -> p a b", b=9)[:, :, 8]).then_inc(dt_act, 1)
            act.wait_ge(dt_dve, 20)
            act.dma_start(tok_scr, tokd[:, :, :, :, :].rearrange("p a b c d -> p a (b c d)")).then_inc(dt_scr, 16)

            act.wait_ge(dt_scr, 48)

            act.wait_ge(hL_ready, 3 * KD)
            def conv_dst(m):
                return bc[:, m, :] if m < 2 else xs[:, m - 2, :]

            with act.Fori(0, SG) as g:
                def conv_silu(m):
                    act.wait_ge(conv_dve, g * 18 + 3 * m + 3)
                    dst = conv_dst(m)
                    act.activation(dst[:, 0:SEQ], cacc[:, 0:SEQ], ACT.Silu)
                    act.activation(dst[:, SEQ:T].rearrange("p (b i) -> p b i", i=DS),
                                   cacc[:, PW:CWID].rearrange("p (b i) -> p b i", i=SW)[:, :, 0:DS],
                                   ACT.Silu).then_inc(conv_done, 1)

                def load_cumrow(c):
                    o, n = chunk(c)
                    act.dma_start(cumrow[c % 2][:, :, 0:n],
                                  cum_scr[ds(g * HG, HG), o:o + n].partition_broadcast(P)).then_inc(cr_in[c % 2], 16)

                def z_part(k):
                    m, c = ZG[k]
                    evac(c, g * SSD_USES + (U_SSD + 7 + m), [(cols(zs[:, m, :], c), gap(c))])

                def copy_in(c):
                    o, n = chunk(c)
                    act.wait_ge(a_ready, g * NCH + c + 1)
                    if c:
                        act.wait_ge(b_ready, g * NT + c)
                    act.copy(xtok[0:n, :], A[0][0:n, :]).then_inc(a_copied, 1)
                    act.copy(bcb[0:n, 0:P + n], A[1][0:n, 0:P + n]).then_inc(a_copied, 1)

                def decay(c):
                    o, n = chunk(c)
                    act.wait_ge(seg_done, g * NCH + c + 1)
                    act.activation(dec[c % 2][0:n, :, 0:n], dec[c % 2][0:n, :, 0:n], ACT.Exp).then_inc(exp_done, 1)
                    if c < NT:
                        if c >= 2:
                            act.wait_ge(d_step, g * DSUM + sum(DSTEPS[:c - 1]))
                        act.activation(elg[:, c % 2, :], cumrow[c % 2][:, :, P - 1], ACT.Exp).then_inc(el_done, 1)
                    if c + 2 < NCH:
                        act.wait_ge(el_done, g * NT + c + 1)
                        load_cumrow(c + 2)

                def load_s0(hp):
                    act.dma_start(s0[hp % 2][:, :, :],
                                  state_ssm[0][:, ds(g * HG + 2 * hp, 2), :, :].rearrange("b h p n -> (h p) b n"))\
                       .then_inc(s0_in[hp % 2], 16)

                load_cumrow(0)
                load_cumrow(1)
                for m in range(6):
                    u = g * SSD_USES + (U_SSD + m + 1)
                    cr = craw[m % 2]
                    if m >= 2:
                        act.wait_ge(conv_dve, g * 18 + 3 * (m - 2) + 3)
                    evac(0, u, [(cr[:, 3:3 + TH[0][1]], gap(0))])
                    evac(1, u, [(cr[:, 3 + TH[1][0]:3 + TH[1][1]], gap(1))])
                    evac(2, u, [(cr[:, 3 + TH[2][0]:3 + SEQ], G[2][:, 0:SEQ - TH[2][0]]),
                                (cr[:, PW:CWID].rearrange("p (b i) -> p b i", i=SW)[:, :, CW - 1:],
                                 G[2][:, SEQ - TH[2][0]:T - TH[2][0]].rearrange("p (b i) -> p b i", i=DS))])
                    if m >= 1:
                        conv_silu(m - 1)
                    act.wait_ge(pad_ready, g * 6 + m + 1)
                    act.wait_ge(g_free[2], u)
                    if m >= 1:
                        act.wait_ge(conv_done, g * 6 + m)
                    act.activation(cacc[:, 0:CWID - 3], cr[:, 3:CWID], ACT.Identity,
                                   bias=ccg[:, m, 28:29], scale=ccg[:, m, 27:28]).then_inc(conv_act, 1)
                decay(0)
                conv_silu(5)
                act.dma_start(nc_scr[ds(g + 16, 1), :, :].rearrange("a p n -> p (a n)"), ncg[:, 0, :]).then_inc(nc_out, 16)
                act.dma_start(nc_scr[ds(g + 20, 1), :, :].rearrange("a p n -> p (a n)"), ncg[:, 1, :]).then_inc(nc_out, 16)
                act.dma_start(nc_scr[ds(g * 4, 4), :, :].rearrange("a p n -> p a n"), ncg[:, 2:6, :]).then_inc(nc_out, 16)

                act.wait_ge(conv_done, g * 6 + 6)
                load_s0(0)
                load_s0(1)
                for k in range(3):
                    z_part(k)
                copy_in(0)
                decay(1)
                for c in range(NCH):
                    z_part(3 + c)
                    if c + 1 < NCH:
                        copy_in(c + 1)
                    if c + 2 < NCH:
                        decay(c + 2)

                for c in range(3):
                    act.wait_ge(g_free[c], g * SSD_USES + (U_SSD + 10))
                for m in range(XT):
                    act.activation(zs[:, m, :], zs[:, m, :], ACT.Silu).then_inc(zs_silu, 1)
                for hp in range(4):
                    act.wait_ge(s0_tr, g * 4 + hp + 1)
                    act.copy(s0t[:, 4:8, :].rearrange("p b n -> p (b n)"), A[4][:, :]).then_inc(s0t_act, 1)
                    act.wait_ge(s0_new, g * 12 + 3 * hp + 3)
                    act.dma_start(ssm_s[0][:, ds(g * HG + 2 * hp, 2), :, :].rearrange("b h p n -> (h p) b n"),
                                  s0[hp % 2][:, :, :]).then_inc(ssm_out, 16)
                    if hp < 2:
                        act.wait_ge(ssm_out, g * 64 + 16 * hp + 16)
                        load_s0(hp + 2)
                act.wait_ge(st_ready, g + 1)
                act.wait_ge(y_ready, g * NCH + NCH)
                act.copy(ytok[:, :], A[4][:, :]).then_inc(st_ev, 1)
                act.wait_ge(st_ev, g + 1)
                act.dma_start(ssm_p[0, 0, ds(g * HG, HG), :, :].rearrange("(a h) p n -> (h p) a n", h=2),
                              ytok[:, :].rearrange("p (a n) -> p a n", n=P)).then_inc(st_out, 16)

                act.wait_ge(ssm_out, g * 64 + 64)
                squares(xs, XT, 0, g * (XT - 1) + KD - 1, lambda f: act.wait_ge(gate_done, g * (XT + 1) + XT + 1))
                roots(XT, g * SSD_USES + (U_SSD + 11))
                act.wait_ge(st_out, g * 16 + 16)
                for k in range(3 * XT):
                    m, c = k % XT, k // XT
                    act.wait_ge(yn_done, g * 3 * XT + k + 1)
                    act.copy(cols(yH[:, m, :], c), cols(xs[:, m, :], c)).then_inc(yH_ready, 1)
            act.wait_ge(acc_add, SG)
            act.dma_start(ba_scr, acc8[:, :, :]).then_inc(ba_out, 16)
            def by_residue(gr, dst, c, hi):
                lo = TH[c][0]
                if gr < 2:
                    return dst[:, lo:hi], G[c][:, 0:hi - lo]
                return (dst.rearrange("p (r a) -> p a r", r=16)[:, lo // 16:hi // 16, :],
                        G[c][:, 0:hi - lo].rearrange("p (a r) -> p a r", r=16))

            def qkv_part(j, gr, i):
                k, c = i // 3, i % 3
                u = j * 9 + (U_ATT + gr * 3 + k + 1)
                dst = qkv[gr][k]
                if c < 2:
                    evac(c, u, [by_residue(gr, dst, c, TH[c][1])])
                else:
                    smp = qkvs[:, k, gr, j, :] if isinstance(j, int) else qkvs[:, k, gr, ds(j, 1), :].rearrange("p a n -> p (a n)")
                    evac(c, u, [by_residue(gr, dst, 2, SEQ),
                                (smp, G[2][:, SEQ - TH[2][0]:T - TH[2][0]])])

            def unit(j, gr, nxt):
                n = j * 24 + 8 * gr
                for i in range(NT + 1):
                    if i < NT:
                        if i == 0:
                            act.wait_ge(unit_out[gr], j * (48, 64, 96)[gr] + 1)
                        act.wait_ge(vt_ready, n + i + 1)
                        kt = k_tile(gr, i)
                        ins = act.copy(vtok[gr][:, i, :], A[0][:, 0:P])
                        if kt is not None:
                            ins = act.copy(ktok[gr][:, kt, :], A[0][:, P:2 * P])
                        ins.then_inc(vt_out, 1)
                        act.wait_ge(s_min, n + i + 3)
                        w = P * len(blocks(gr, i))
                        for s in range(2):
                            ins = act.activation(sbuf[i % 2][:, s, 0:w], sbuf[i % 2][:, s, 0:w], ACT.Exp, scale=-1.0,
                                                 bias=obuf[gr][:, i, 128 + s:129 + s], accum_out=obuf[gr][:, i, 130 + s:131 + s])
                        ins.then_inc(p_done, 1)
                    if nxt is not None:
                        qkv_part(*nxt, i)

            for i in range(9):
                qkv_part(0, 0, i)
            with act.Fori(0, NJ - 1) as j:
                unit(j, 0, (j, 1))
                unit(j, 1, (j, 2))
                unit(j, 2, (j + 1, 0))
            unit(NJ - 1, 0, (NJ - 1, 1))
            unit(NJ - 1, 1, (NJ - 1, 2))
            unit(NJ - 1, 2, None)
            def gates_in(b):
                for k in range(2):
                    u = b * 3 + (U_SAM + 1 + k)
                    for c in range(3):
                        w = TH[c][1] - TH[c][0]
                        act.wait_ge(gate_out[c], b * 32 + (16 * k + 1))
                        act.wait_ge(g_ready[c], u)
                        act.activation(gpart[c][:, 0:w], gap(c), ACT.Sigmoid).then_inc(g_free[c], 1)
                        act.wait_ge(g_free[c], u)
                        act.dma_start(gate_scr[k, ds(b, 1), :, TH[c][0]:TH[c][1]].rearrange("a p n -> p (a n)"),
                                      gpart[c][:, 0:w]).then_inc(gate_out[c], 16)

            for q in gate_out:
                act.sem_inc(q, 1)
            gates_in(0)
            for j in range(NJ):
                act.wait_ge(mg, 11 * j + 3)
                act.activation(marg[:, :, :, :], marg[:, :, :, :], ACT.Exp).then_inc(mg_exp, 1)
                act.wait_ge(mt_ready, j + 1)
                for i in range(2):
                    act.copy(aH[:, j, 512 * i:512 * i + 512], A[2 * (j % 2) + i][:, :]).then_inc(aH_ready, 1)
            for gr in range(NG):
                act.wait_ge(kvn_ps, gr + 1)
                if gr:
                    act.wait_ge(kvn_out, 32 * gr)
                for kv in range(2):
                    act.copy(kvn[:, kv, :], A[kv][0:NS, :]).then_inc(kvn_ev, 1)

            def keys_in(b):
                for j in range(NJ):
                    for i in (1, 2):
                        act.wait_ge(k_fill, b * 12 + 3 * j + i + 1)
                        if not (isinstance(b, int) and 4 * b + j < 2):
                            act.wait_ge(sc_done, b * NJ + j)
                        lo, hi = (512, 1024) if i == 1 else (1024, 1152)
                        act.copy(ktr[j % 2][:, lo:hi], A[(3 * j + i) % 4][:, 0:hi - lo]).then_inc(kt_act, 1)

            def expo(b):
                act.wait_ge(sm_dve, b * 3 + 1)
                act.activation(sS[:, :], sS[:, :], ACT.Exp, scale=-1.0, bias=nm3[:, 3:4], accum_out=sden[:, 0:1]).then_inc(sm_exp, 1)

            def probs_in(b):
                act.wait_ge(sp_ready, b + 1)
                act.copy(pts[:, 8, :], A[1][:, 0:NS])
                act.copy(pts[0:24, 9, :], A[1][0:24, NS:2 * NS]).then_inc(spt_act, 1)

            keys_in(0)
            expo(0)
            with act.Fori(0, DB - 1) as b:
                gates_in(b + 1)
                keys_in(b + 1)
                probs_in(b)
                expo(b + 1)
            probs_in(DB - 1)
            act.wait_ge(aS_out, DB + 1)
            act.copy(aH[:, :, SEQ:T], aS[:, :, :]).then_inc(aH_ready, 1)

            act.wait_ge(mix_step, 9 * KD)
            for c in range(3):
                for f in range(KD):
                    act.copy(cols(hH[:, f, :], c), cols(acc8[:, f, :], c)).then_inc(hH_ready, 1)
            for m in range(KD):
                for c in range(3):
                    evac(c, U_OUT + m + 1, [(cols(m2[:, m, :], c), gap(c))])
            for c in range(3):
                act.wait_ge(g_free[c], U_OUT + KD)
            squares(m2, KD, 24, 19)
            roots(KD, U_NORME)
            squares(x1, KD, 32, 26, lambda f: act.wait_ge(x1_done, 2 * f + 2))
            roots(KD, U_NORMF)
            halves(3 * KD)
            act.wait_ge(hL_ready, 72)

            def hidden(k, u):
                par = k_par(k)
                for i in range(2):
                    for c in range(3):
                        act.wait_ge(uL_ready, k * 2 + i + 1)
                        act.wait_ge(g_ready[c], u + 2 * i + 1)
                        act.activation(cols(sq[i], c), gap(c), ACT.Silu).then_inc(g_free[c], 1)
                    for c in range(3):
                        act.wait_ge(g_free[c], u + 2 * i + 2)
                    act.copy(uH[par][:, i, :], sq[i][:, :]).then_inc(uH_ready, 1)

            k_even = [True]

            def k_par(k):
                k_even[0] = not k_even[0]
                return 1 if k_even[0] else 0

            hidden(0, U_FF)
            with act.Fori(0, 5) as i:
                hidden(i * 2 + 1, i * 24 + (U_FF + 4))
                hidden(i * 2 + 2, i * 24 + (U_FF + 16))
            act.wait_ge(add_done, 1)
            squares(m2, KD, 40, 33)
            roots(KD, U_NORML)
            for q in range(6):
                act.wait_ge(nct_ready, q + 1)
                act.copy(ncrow[:, 512 * q:512 * q + 512], A[4][0:27, :]).then_inc(nct_ev, 1)
            act.wait_ge(nct_ev, 6)
            act.dma_start(conv_p[0, 0], ncrow[0:3, :]).then_inc(nct_out, 16)
            act.dma_start(conv_s[0].rearrange("b i n -> (b i) n"), ncrow[3:27, :]).then_inc(nct_out, 16)
            for t in range(9):
                r = P if t < NT else NS
                act.wait_ge(yt_ready, t + 1)
                if t >= 2:
                    act.wait_ge(y_out[t % 2], 16 * (t // 2))
                act.copy(yo[t % 2][0:r, 0:512], A[2 * (t % 2)][0:r, :]).then_inc(yo_act, 1)
                act.wait_ge(yo_act, t + 1)
                act.wait_ge(yo_dve, t + 1)
                dst = y_prompt[0, t * P:(t + 1) * P, :] if t < NT else y_sample.rearrange("b s d -> (b s) d")
                act.dma_start(dst, yo[t % 2][0:r, :]).then_inc(y_out[t % 2], 16)

        @block.vector
        def _(dve):
            def norm_halves(src, w, u, rbase, base):
                steps = [(c, f) for c in range(3) for f in range(KD)]

                def low(k):
                    c, f = steps[k]
                    dve.wait_ge(hH_ready, base + k + 1)
                    dve.tensor_tensor(cols(hL[:, f, :], c), hv(k, c), cols(hH[:, f, :], c).bitcast(F32),
                                      ALU.subtract).then_inc(hL_ready, 1)

                for k, (c, f) in enumerate(steps):
                    if f == 0:
                        dve.wait_ge(g_free[c], u)
                        dve.reciprocal(cols(rs, c), cols(rs, c)).then_inc(rs_ready, 1)
                        dve.wait_ge(rs_ready, rbase + c + 1)
                    dve.scalar_tensor_tensor(out=hv(k, c), in0=cols(src[:, f, :], c), scalar=nrm[:, w + f:w + f + 1],
                                             in1=cols(rs, c), op0=ALU.mult, op1=ALU.mult).then_inc(hv_ready, 1)
                    if k >= 1:
                        low(k - 1)
                low(len(steps) - 1)

            dve.sem_inc(yL_ready, 1)
            dve.sem_inc(nc_out, 1)
            dve.wait_ge(par_ps, 1)
            for i in range(2):
                dve.tensor_copy(ccd[:, 12 * i:12 * i + 12, 0:24], A[i][:, 0:288].rearrange("p (a b) -> p a b", b=24)).then_inc(par_out, 1)
            dve.tensor_copy(nrm[:, :], A[2][:, 0:48]).then_inc(par_out, 1)
            dve.tensor_copy(ccd[:, :, 24:29], A[2][:, 64:184].rearrange("p (a b) -> p a b", b=5)).then_inc(par_out, 1)
            for f in range(KD):
                b1, b2 = (A[1], A[2]) if f % 2 == 0 else (A[4], G[0])
                dve.wait_ge(xt_ps, f + 1)
                dve.tensor_copy(acc8[:, f, 512:SEQ], b1[:, :])
                dve.tensor_copy(acc8[:, f, SEQ:T], b2[:, 0:NS]).then_inc(xt_dve, 1)
            norm_halves(acc8, 0, U_NORM0, 0, 0)

            s = [0]

            def step(ins):
                s[0] += 1
                ins.then_inc(dt_dve, 1)
                dve.wait_ge(dt_dve, s[0])

            dve.wait_ge(dt_act, 3)
            step(dve.tensor_scalar(du[:, :], de[:, :], 1.0, None, ALU.add))
            step(dve.tensor_scalar(dr[:, :], du[:, :], -1.0, 1e-30, ALU.add, ALU.max))
            step(dve.reciprocal(dr[:, :], dr[:, :]))
            dve.wait_ge(dt_act, 4)
            step(dve.tensor_tensor(dl[:, :], dl[:, :], de[:, :], ALU.mult))
            step(dve.tensor_tensor(dl[:, :], dl[:, :], dr[:, :], ALU.mult))
            step(dve.tensor_scalar(du[:, :], du[:, :], 1.0, None, ALU.is_equal))
            step(dve.tensor_tensor(du[:, :], du[:, :], de[:, :], ALU.mult))
            step(dve.tensor_tensor(dl[:, :], dl[:, :], du[:, :], ALU.add))
            step(dve.scalar_tensor_tensor(out=dv[:, :], in0=dv[:, :], scalar=0.0, in1=dl[:, :], op0=ALU.max, op1=ALU.add))
            step(dve.tensor_scalar(du[:, :], dv[:, :], hcol[:, 2:3], -1.0, ALU.mult, ALU.mult))
            step(dve.memset(dr[:, :], 1.0))
            step(dve.memset(dr[:, 0:SEQ:P], 0.0))
            step(dve.memset(dr[:, SEQ:T:DS], 0.0))
            step(dve.tensor_tensor_scan(dcum[:, :], dr[:, :], du[:, :], 0.0, ALU.mult, ALU.add))
            for o, n, w in ((0, NT, P), (SEQ, DB, DS)):
                cv = dcum[:, o:o + n * w].rearrange("h (n w) -> h n w", w=w)
                step(dve.tensor_tensor(de[:, o:o + n * w].rearrange("h (n w) -> h n w", w=w),
                                       cv[:, :, w - 1:w].to_broadcast([SH, n, w]), cv, ALU.subtract))
            dve.tensor_copy(rhsx[:, 0:8], dcum[:, SEQ + DS - 1:T:DS]).then_inc(dt_dve, 1)
            dve.wait_ge(dt_act, 6)
            dve.tensor_tensor(de[:, :], de[:, :], dv[:, :], ALU.mult).then_inc(dt_dve, 1)
            dve.wait_ge(dt_ps, 2)
            dve.memset(tokd[:, :, :, :, :], 0.0).then_inc(dt_dve, 1)
            dve.wait_ge(dt_dve, 19)
            for i, (t0, n, r) in enumerate(((0, 4, P), (4, 4, P), (8, 1, NS))):
                ins = dve.tensor_copy(tokd[0:r, :, t0:t0 + n, :, :].rearrange("p g t k e -> p g (t k) e"),
                                      A[i][0:r, 0:n * P].rearrange("p (a g e) -> p g a e", g=SG, e=HG))
            ins.then_inc(dt_dve, 1)
            dve.wait_ge(dt_act, 8)
            dve.wait_ge(consts, 5)
            dskg, sng, eclg = small[:, 32:36], small[:, 36:40], small[:, 40:72].rearrange("p (a b) -> p a b", b=DB)
            with dve.Fori(0, SG) as g:
                dve.wait_ge(cc_in, g * 48 + 48)
                dve.tensor_copy(dskg, dsk[:, ds(g * 4, 4)])
                dve.tensor_copy(sng, nrm[:, ds(g * 4 + 32, 4)])
                dve.tensor_copy(eclg, ecl[:, ds(g * 4, 4), :]).then_inc(grp, 1)
                dve.wait_ge(grp, g + 1)
                dve.wait_ge(nc_out, g * 48 + 1)
                def seg(c):
                    o, n = chunk(c)
                    dve.wait_ge(cr_in[c % 2], g * (80 if c % 2 == 0 else 64) + 16 * (c // 2 + 1))
                    if c >= 2:
                        dve.wait_ge(b_ready, g * NT + c - 1)
                    mask = smask if n == P else smaskS
                    for h in range(HG):
                        ins = dve.scalar_tensor_tensor(out=dec[c % 2][0:n, h, 0:n], in0=cumrow[c % 2][0:n, h, 0:n],
                                                       scalar=tokg[0:n, c, 0, h:h + 1], in1=mask[0:n, 0:n],
                                                       op0=ALU.subtract, op1=ALU.add)
                    ins.then_inc(seg_done, 1)

                for m in range(6):
                    if m == 5:
                        dve.wait_ge(tok_in, g * 16 + 16)
                        seg(0)
                    cr, u = craw[m % 2], g * SSD_USES + (U_SSD + m + 1)
                    smp = cr[:, PW:CWID].rearrange("p (b i) -> p b i", i=SW)
                    dve.wait_ge(g_ready[0], u)
                    dve.memset(cr[:, 0:3], 0.0)
                    dve.tensor_copy(smp[:, :, 0:3], ccg[:, m, 0:24].rearrange("p (b i) -> p b i", i=3)).then_inc(pad_ready, 1)
                    dve.wait_ge(g_free[2], u)
                    dve.tensor_copy(ncg[:, m, 0:3], cr[:, SEQ:SEQ + 3])
                    dve.tensor_copy(ncg[:, m, 3:27].rearrange("p (b i) -> p b i", i=3), smp[:, :, SW - 3:SW])
                    dve.wait_ge(conv_act, g * 6 + m + 1)
                    dve.wait_ge(pad_ready, g * 6 + m + 1)
                    for k, i in enumerate((2, 1, 0)):
                        if k:
                            dve.wait_ge(conv_dve, g * 18 + 3 * m + k)
                        dve.scalar_tensor_tensor(out=cacc[:, 0:CWID - 3], in0=cr[:, i:i + CWID - 3],
                                                 scalar=ccg[:, m, 24 + i:25 + i], in1=cacc[:, 0:CWID - 3],
                                                 op0=ALU.mult, op1=ALU.add).then_inc(conv_dve, 1)
                def weigh(c):
                    o, n = chunk(c)
                    dve.wait_ge(exp_done, g * NCH + c + 1)
                    dve.wait_ge(a_copied, g * 2 * NCH + 2 * c + 2)
                    for h in range(HG):
                        ins = dve.scalar_tensor_tensor(out=dec[c % 2][0:n, h, 0:n], in0=dec[c % 2][0:n, h, 0:n],
                                                       scalar=tokg[0:n, c, 1, h:h + 1], in1=bcb[0:n, P:P + n],
                                                       op0=ALU.mult, op1=ALU.mult)
                    ins.then_inc(w_done, 1)

                def heads(a):
                    return a.rearrange("p (h e) -> p h e", e=64)

                def combine(c):
                    o, n = chunk(c)
                    b = g * DSUM + sum(DSTEPS[:c])
                    if c < NT:
                        dve.wait_ge(b_ready, g * NT + c + 1)
                    if c == 0:
                        dve.tensor_copy(ytok[:, :], A[2][:, :]).then_inc(d_step, 1)
                        dve.tensor_copy(st[:, :], A[4][:, :]).then_inc(d_step, 1)
                        return
                    dve.tensor_tensor(heads(ytok[0:n, :]), heads(A[3][0:n, :]),
                                      tokg[0:n, c, 3, :].unsqueeze(2).to_broadcast([n, HG, 64]), ALU.mult).then_inc(d_step, 1)
                    if c < NT:
                        dve.wait_ge(el_done, g * NT + c + 1)
                        dve.tensor_tensor(heads(st[:, :]), heads(st[:, :]),
                                          elg[:, c % 2, :].unsqueeze(2).to_broadcast([P, HG, 64]), ALU.mult).then_inc(d_step, 1)
                    dve.wait_ge(d_step, b + 1)
                    dve.tensor_tensor(ytok[0:n, :], ytok[0:n, :], A[2][0:n, :], ALU.add).then_inc(d_step, 1)
                    if c < NT:
                        dve.wait_ge(d_step, b + 3)
                        dve.tensor_tensor(st[:, :], st[:, :], A[4][:, :], ALU.add).then_inc(d_step, 1)

                def add_skip(c):
                    o, n = chunk(c)
                    dve.wait_ge(y_ready, g * NCH + c + 1)
                    for m in range(XT):
                        ins = dve.scalar_tensor_tensor(out=xs[:, m, o:o + n], in0=xs[:, m, o:o + n],
                                                       scalar=dskg[:, m:m + 1], in1=A[0][:, m * n:(m + 1) * n],
                                                       op0=ALU.mult, op1=ALU.add)
                    ins.then_inc(yev_done, 1)

                dve.wait_ge(conv_done, g * 6 + 6)
                seg(1)
                weigh(0)
                for c in range(NT):
                    combine(c)
                    weigh(c + 1)
                    if c + 2 < NCH:
                        seg(c + 2)
                    if c == NT - 1:
                        dve.memset(cm[:, :], 0.0).then_inc(cmbm, 1)
                        dve.tensor_tensor(bm[:, :, :], bcb[0:NS, 0:P].unsqueeze(1).to_broadcast([NS, DB, P]),
                                          bmask[:, :].unsqueeze(2).to_broadcast([NS, DB, P]), ALU.mult).then_inc(cmbm, 1)
                        dve.wait_ge(cmbm, g * 3 + 1)
                        dve.tensor_copy(cm[:, :].rearrange("p (b i) -> p b i", i=72)[:, :, 0:DS],
                                        bc[:, 1, SEQ:T].rearrange("p (b i) -> p b i", i=DS)).then_inc(cmbm, 1)
                    add_skip(c)
                for hp in range(4):
                    s = s0[hp % 2]
                    dve.wait_ge(s0_tr, g * 4 + hp + 1)
                    dve.tensor_copy(s0t[:, 0:4, :].rearrange("p b n -> p (b n)"), A[1][:, :]).then_inc(s0t_dve, 1)
                    dve.tensor_tensor(s[:, :, :], s[:, :, :], eclg[:, hp, :].unsqueeze(2).to_broadcast([P, DB, P]),
                                      ALU.mult).then_inc(s0_new, 1)
                    if hp == 0:
                        dve.wait_ge(yev_done, g * NCH + NT)
                    dve.wait_ge(zs_silu, g * XT + hp + 1)
                    dve.tensor_tensor(xs[:, hp, 0:SEQ], xs[:, hp, 0:SEQ], zs[:, hp, 0:SEQ], ALU.mult).then_inc(gate_done, 1)
                    dve.wait_ge(s0_new, g * 12 + 3 * hp + 1)
                    dve.wait_ge(s0_up, g * 4 + hp + 1)
                    for i in range(2):
                        dve.tensor_tensor(s[:, 4 * i:4 * i + 4, :].rearrange("p b n -> p (b n)"),
                                          s[:, 4 * i:4 * i + 4, :].rearrange("p b n -> p (b n)"),
                                          A[1 + 3 * i][:, :], ALU.add).then_inc(s0_new, 1)
                combine(NT)
                add_skip(NT)
                dve.wait_ge(yev_done, g * NCH + NCH)
                dve.tensor_tensor(xs[:, :, SEQ:T], xs[:, :, SEQ:T], zs[:, :, SEQ:T], ALU.mult).then_inc(gate_done, 1)

                def low(k):
                    m, c = k % XT, k // XT
                    dve.wait_ge(yH_ready, g * 3 * XT + k + 1)
                    dve.tensor_tensor(cols(yL[:, m, :], c), cols(xs[:, m, :], c), cols(yH[:, m, :], c).bitcast(F32),
                                      ALU.subtract).then_inc(yL_ready, 1)

                dve.wait_ge(gate_done, g * (XT + 1) + XT + 1)
                for k in range(3 * XT):
                    m, c = k % XT, k // XT
                    if m == 0:
                        dve.wait_ge(g_free[c], g * SSD_USES + (U_SSD + 11))
                        dve.reciprocal(cols(rs, c), cols(rs, c)).then_inc(rs_ready, 1)
                        dve.wait_ge(rs_ready, g * 3 + (4 + c))
                    dve.scalar_tensor_tensor(out=cols(xs[:, m, :], c), in0=cols(xs[:, m, :], c), scalar=sng[:, m:m + 1],
                                             in1=cols(rs, c), op0=ALU.mult, op1=ALU.mult).then_inc(yn_done, 1)
                    if k >= 1:
                        low(k - 1)
                low(3 * XT - 1)
                dve.wait_ge(acc_zero, 1)
                for m in range(KD):
                    for c in range(3):
                        dve.wait_ge(g_ready[c], g * SSD_USES + (U_SSD + 12 + m))
                        dve.tensor_tensor(cols(acc8[:, m, :], c), cols(acc8[:, m, :], c), gap(c), ALU.add).then_inc(g_free[c], 1)
                dve.drain().then_inc(acc_add, 1)
            dve.wait_ge(amask, 2)

            def unit(j, gr):
                n = j * 24 + 8 * gr
                for i in range(NT + 2):
                    if i < NT:
                        if i == 0:
                            dve.wait_ge(unit_out[gr], j * (48, 64, 96)[gr] + 1)
                        dve.wait_ge(s_ready, n + i + 1)
                        alone(dve)
                        w = P * len(blocks(gr, i))
                        mask = mask2[:, :] if gr == 2 else mask01[:, 256 - w:256]
                        for s in range(2):
                            ins = dve.tensor_tensor_reduce(sbuf[i % 2][:, s, 0:w], A[1 + s][:, 0:w], mask,
                                                           -ASC, 3e38, ALU.add, ALU.min, obuf[gr][:, i, 128 + s:129 + s])
                        ins.then_inc(s_min, 1)
                    if 1 <= i <= NT:
                        w = 2 * P * len(blocks(gr, i - 1))
                        dve.wait_ge(pt_ready, n + i)
                        dve.tensor_copy(pt[(i - 1) % 2][:, :, :].rearrange("p a b -> p (a b)")[:, 0:w], A[3][:, 0:w]).then_inc(pt_out, 1)
                    if i >= 2:
                        dve.wait_ge(pv_ready, n + i - 1)
                        dve.tensor_copy(obuf[gr][:, i - 2, 0:P], A[4][:, 0:P]).then_inc(ob_out, 1)

            with dve.Fori(0, NJ) as j:
                for gr in range(NG):
                    unit(j, gr)
            for j in range(NJ):
                v = mb[j % 2]
                s = [11 * j]

                def mstep(ins):
                    s[0] += 1
                    ins.then_inc(mg, 1)
                    dve.wait_ge(mg, s[0])

                dve.wait_ge(mb_in[j % 2], 48 * (j // 2 + 1))
                nm, den = v[:, :, :, 128:130], v[:, :, :, 130:132]
                mstep(dve.tensor_tensor(mmin[:, :, :], nm[:, :, 0, :], nm[:, :, 1, :], ALU.min))
                mstep(dve.tensor_tensor(mmin[:, :, :], mmin[:, :, :], nm[:, :, 2, :], ALU.min))
                mstep(dve.tensor_tensor(marg[:, :, :, :], mmin[:, :, :].unsqueeze(2).to_broadcast([P, NT, NG, 2]), nm, ALU.subtract))
                dve.wait_ge(mg_exp, j + 1)
                mstep(dve.tensor_tensor(mwd[:, :, :, :], marg[:, :, :, :], den, ALU.mult))
                mstep(dve.tensor_tensor(mden[:, :, :], mwd[:, :, 0, :], mwd[:, :, 1, :], ALU.add))
                mstep(dve.tensor_tensor(mden[:, :, :], mden[:, :, :], mwd[:, :, 2, :], ALU.add))
                mstep(dve.reciprocal(mden[:, :, :], mden[:, :, :]))
                mstep(dve.tensor_tensor(marg[:, :, :, :], marg[:, :, :, :], mden[:, :, :].unsqueeze(2).to_broadcast([P, NT, NG, 2]), ALU.mult))
                o4 = v[:, :, :, 0:P].rearrange("p i g (s e) -> p (i g) s e", e=64)
                mstep(dve.tensor_tensor(o4, o4, marg[:, :, :, :].rearrange("p i g s -> p (i g) s").unsqueeze(3)
                                        .to_broadcast([P, NT * NG, 2, 64]), ALU.mult))
                mstep(dve.tensor_tensor(v[:, :, 0, 0:P], v[:, :, 0, 0:P], v[:, :, 1, 0:P], ALU.add))
                mstep(dve.tensor_tensor(v[:, :, 0, 0:P], v[:, :, 0, 0:P], v[:, :, 2, 0:P], ALU.add))
                for i in range(2):
                    dve.wait_ge(aH_ready, 2 * j + i + 1)
                    part = slice(512 * i, 512 * i + 512)
                    dve.tensor_tensor(aL[:, j, part], A[2 * (j % 2) + i][:, :], aH[:, j, part].bitcast(F32), ALU.subtract).then_inc(aL_ready, 1)

            def keys_in(b):
                for j in range(NJ):
                    dve.wait_ge(k_fill, b * 12 + 3 * j + 1)
                    if not (isinstance(b, int) and 4 * b + j < 2):
                        dve.wait_ge(sc_done, b * NJ + j)
                    dve.tensor_copy(ktr[j % 2][:, 0:512], A[3 * j % 4][:, :]).then_inc(kt_dve, 1)

            def softmax(b):
                u = b * 3 + (U_SAM + 3)
                if not isinstance(b, int):
                    dve.wait_ge(sp_ready, b)
                for c, (lo, hi) in enumerate(((0, 152), (152, 664), (664, 1176))):
                    dve.wait_ge(g_ready[c], u)
                    alone(dve)
                    dve.tensor_tensor_reduce(sS[:, lo:hi], G[c][0:NS, 0:hi - lo], maskS[:, lo:hi], -ASC, 3e38,
                                             ALU.add, ALU.min, nm3[:, c:c + 1]).then_inc(g_free[c], 1)
                for c in range(3):
                    dve.wait_ge(g_free[c], u)
                dve.tensor_reduce(nm3[:, 3:4], nm3[:, 0:3], AX.X, ALU.min).then_inc(sm_dve, 1)
                dve.wait_ge(sm_exp, b + 1)
                dve.reciprocal(sden[:, 1:2], sden[:, 0:1]).then_inc(sm_dve, 1)
                dve.wait_ge(sm_dve, b * 3 + 2)
                dve.tensor_scalar(sS[:, :], sS[:, :], sden[:, 1:2], None, ALU.mult).then_inc(sm_dve, 1)

            def probs_in(b):
                dve.wait_ge(sp_ready, b + 1)
                dve.tensor_copy(pts[:, 0:8, :].rearrange("p a b -> p (a b)"), A[0][:, :]).then_inc(spt_dve, 1)

            def out_in(b):
                dve.wait_ge(spv_ready, b + 1)
                for s in range(2):
                    ins = dve.tensor_copy(aS[64 * s:64 * s + 64, :, ds(b * DS, DS)],
                                          A[4][64 * s:64 * s + 64, 0:64].rearrange("p (j s q) -> p s j q", s=2, q=DS)[:, s, :, :])
                ins.then_inc(aS_out, 1)

            dve.wait_ge(mS_in, 16)
            keys_in(0)
            softmax(0)
            with dve.Fori(0, DB - 1) as b:
                keys_in(b + 1)
                probs_in(b)
                softmax(b + 1)
                out_in(b)
            probs_in(DB - 1)
            out_in(DB - 1)
            dve.wait_ge(aH_ready, 9)
            dve.wait_ge(aS_out, DB + 1)
            dve.tensor_tensor(aL[:, :, SEQ:T], aS[:, :, :], aH[:, :, SEQ:T].bitcast(F32), ALU.subtract).then_inc(aL_ready, 1)

            for m in range(KD):
                dve.wait_ge(mix_in[m], 48)
                for c in range(3):
                    part, ga, n = cols(acc8[:, m, :], c), cols(gates[0][:, m, :], c), 9 * m + 3 * c
                    dve.tensor_tensor(part, part, cols(gates[1][:, m, :], c), ALU.mult).then_inc(mix_step, 1)
                    dve.wait_ge(g_ready[c], U_PROJ + m + 1)
                    dve.tensor_tensor(ga, ga, gap(c), ALU.mult).then_inc(g_free[c], 1)
                    dve.wait_ge(g_free[c], U_PROJ + m + 1)
                    dve.wait_ge(mix_step, n + 1)
                    dve.tensor_tensor(part, part, ga, ALU.add).then_inc(mix_step, 2)
            for k, (c, f) in enumerate([(c, f) for c in range(3) for f in range(KD)]):
                dve.wait_ge(hH_ready, 24 + k + 1)
                dve.tensor_tensor(cols(hL[:, f, :], c), cols(acc8[:, f, :], c), cols(hH[:, f, :], c).bitcast(F32),
                                  ALU.subtract).then_inc(hL_ready, 1)

            dve.wait_ge(xt_in, 16)
            for c in range(3):
                dve.wait_ge(g_free[c], U_NORME)
                dve.reciprocal(cols(rs, c), cols(rs, c)).then_inc(rs_ready, 1)
            dve.wait_ge(rs_ready, 18)
            for f in range(KD):
                dve.scalar_tensor_tensor(out=m2[:, f, :], in0=m2[:, f, :], scalar=nrm[:, 8 + f:9 + f], in1=rs[:, :],
                                         op0=ALU.mult, op1=ALU.mult).then_inc(x1_done, 1)
                dve.wait_ge(x1_done, 2 * f + 1)
                dve.tensor_tensor(x1[:, f, :], x1[:, f, :], m2[:, f, :], ALU.add).then_inc(x1_done, 1)
            dve.wait_ge(x1_done, 2 * KD)
            norm_halves(x1, 16, U_NORMF, 18, 48)

            dve.wait_ge(facc_zero, 1)

            def hidden(k, par, u):
                for i in range(2):
                    for c in range(3):
                        dve.wait_ge(g_free[c], u + 2 * i + 1)
                        dve.wait_ge(g_ready[c], u + 2 * i + 2)
                        dve.tensor_tensor(cols(sq[i], c), cols(sq[i], c), gap(c), ALU.mult).then_inc(g_free[c], 1)
                    dve.wait_ge(uH_ready, k * 2 + i + 1)
                    dve.tensor_tensor(uL[par][:, i, :], sq[i][:, :], uH[par][:, i, :].bitcast(F32), ALU.subtract).then_inc(uL_ready, 1)

            def collect(u):
                for m in range(KD):
                    for c in range(3):
                        dve.wait_ge(g_ready[c], u + m + 1)
                        dve.tensor_tensor(cols(m2[:, m, :], c), cols(m2[:, m, :], c), gap(c), ALU.add).then_inc(g_free[c], 1)

            dve.sem_inc(uL_ready, 2)
            hidden(0, 0, U_FF)
            with dve.Fori(0, 5) as i:
                hidden(i * 2 + 1, 1, i * 24 + (U_FF + 4))
                collect(i * 24 + (U_FF + 8))
                hidden(i * 2 + 2, 0, i * 24 + (U_FF + 16))
                collect(i * 24 + (U_FF + 20))
            collect(U_FF + 124)
            dve.drain().then_inc(add_done, 1)
            dve.wait_ge(add_done, 1)
            for c in range(3):
                dve.wait_ge(g_free[c], U_NORML)
                dve.reciprocal(cols(rs, c), cols(rs, c)).then_inc(rs_ready, 1)
                dve.wait_ge(rs_ready, 22 + c)
                for f in range(KD):
                    part, n = cols(m2[:, f, :], c), 2 * (KD * c + f)
                    dve.scalar_tensor_tensor(out=part, in0=part, scalar=nrm[:, 24 + f:25 + f], in1=cols(rs, c),
                                             op0=ALU.mult, op1=ALU.mult).then_inc(y_done, 1)
                    dve.wait_ge(y_done, n + 1)
                    dve.tensor_tensor(cols(x1[:, f, :], c), cols(x1[:, f, :], c), part, ALU.add).then_inc(y_done, 1)
            for t in range(9):
                r = P if t < NT else NS
                dve.wait_ge(yt_ready, t + 1)
                if t >= 2:
                    dve.wait_ge(y_out[t % 2], 16 * (t // 2))
                dve.tensor_copy(yo[t % 2][0:r, 512:D], A[2 * (t % 2) + 1][0:r, :]).then_inc(yo_dve, 1)

        @block.tensor
        def _(pe):
            def bank(c, u):
                pe.wait_ge(g_free[c], u - 1)

            def product(c, u, slot, kt, w, m0, mw, mH, mL, first=False):
                if not first:
                    bank(c, u)
                last = None
                for k in range(kt):
                    hi = wH[slot][:, k * w + m0:k * w + m0 + mw]
                    lo = wL[slot][:, k * w + m0:k * w + m0 + mw]
                    pe.matmul(gap(c, mw), hi, cols(mH[:, k, :], c), start=k == 0, stop=False)
                    pe.matmul(gap(c, mw), hi, cols(mL[:, k, :], c), start=False, stop=False)
                    last = pe.matmul(gap(c, mw), lo, cols(mH[:, k, :], c), start=False, stop=k == kt - 1)
                last.then_inc(g_ready[c], 1)

            def sums(n, u, base, first=False):
                for f in range(n):
                    pe.wait_ge(sq_ready, base + f + 1)
                    for c in range(3):
                        if f == 0 and not first:
                            bank(c, u)
                        mm = pe.matmul(gap(c), ones[:, :], cols(sq[f % 2], c), start=f == 0, stop=f == n - 1)
                        if f == n - 1:
                            mm.then_inc(g_ready[c], 1)
                        elif c == 2:
                            mm.then_inc(sq_used, 1)

            pe.wait_ge(consts, 1)
            pe.wait_ge(par_in, 16 * 8)
            for k in range(CT):
                pe.transpose(A[k // 12][:, 24 * (k % 12):24 * (k % 12) + 24], strows[:, k * P:(k + 1) * P], ident[0:24, 0:24])
                pe.transpose(A[2][:, 64 + 5 * k:69 + 5 * k], convrows[:, k * P:(k + 1) * P], ident[0:5, 0:5])
            pe.transpose(A[2][:, 0:48], rows48[:, :], ident[0:48, 0:48]).then_inc(par_ps, 1)
            pe.wait_ge(x_in, 32)
            pe.wait_ge(par_out, 4)
            for f in range(KD):
                b = [A[0], A[1], A[2]] if f % 2 == 0 else [A[3], A[4], G[0]]
                if f >= 2:
                    pe.wait_ge(xt_act, f - 1)
                    pe.wait_ge(xt_dve, f - 1)
                for i in range(NT):
                    pe.transpose(b[i // 4][:, (i % 4) * P:(i % 4 + 1) * P], xin[:, i, f * P:(f + 1) * P], ident[:, :])
                pe.transpose(b[2][:, 0:NS], xins[:, f * P:(f + 1) * P], ident[0:NS, 0:NS]).then_inc(xt_ps, 1)
            pe.wait_ge(xt_dve, KD)
            sums(KD, U_NORM0, 0, first=True)
            pe.wait_ge(w_split, 2)
            for c in range(3):
                pe.wait_ge(hL_ready, KD * (c + 1))
                product(c, U_DT, 0, KD, SH, 0, SH, hH, hL)
            pe.wait_ge(dt_dve, 17)
            pe.wait_ge(consts, 5)
            pe.wait_ge(col_in, 48)
            for a in range(16):
                mm = pe.matmul(A[3][:, 9 * a:9 * a + 9], dtsel[:, a, :], rhsx[:, :], start=True, stop=True)
            mm.then_inc(dt_ps, 1)
            pe.wait_ge(dt_dve, 18)
            pe.wait_ge(dt_act, 6)
            for t in range(9):
                o, n = (t * P, P) if t < NT else (SEQ, NS)
                for k, src in enumerate((dcum, dv, de, dl)):
                    mm = pe.transpose(A[t // 4][0:n, (t % 4) * P + k * SH:(t % 4) * P + k * SH + SH], src[:, o:o + n], ident[0:SH, 0:SH])
            mm.then_inc(dt_ps, 1)

            with pe.Fori(0, SG) as g:
                def tile(k, mH, mL, kt, u, only=None):
                    slot = (C_SSD + k) % SPL
                    if only in (None, 0):
                        pe.wait_ge(w_split, g * SSD_CH + (C_SSD + k + 2))
                    for c in (range(3) if only is None else [only]):
                        product(c, u, slot, kt, P, 0, P, mH, mL)

                def use(k):
                    return g * SSD_USES + (U_SSD + k)

                for k in range(6):
                    tile(k, hH, hL, KD, use(k + 1))

                def z_part(i):
                    m, c = ZG[i]
                    tile(6 + m, hH, hL, KD, use(7 + m), only=c)

                def by_token(c):
                    o, n = chunk(c)
                    if c == 0:
                        pe.wait_ge(conv_done, g * 6 + 6)
                        pe.wait_ge(dt_dve, 20)
                    if c >= 2:
                        pe.wait_ge(yev_done, g * NCH + c - 1)
                    if c == NT:
                        alone(pe)
                    for m in range(XT):
                        pe.transpose(A[0][0:n, m * P:(m + 1) * P], xs[:, m, o:o + n], ident[:, :])
                    pe.transpose(A[1][0:n, 0:P], bc[:, 0, o:o + n], ident[:, :])
                    pe.matmul(A[1][0:n, P:P + n], bc[:, 0, o:o + n], bc[:, 1, o:o + n], start=True, stop=True)\
                      .then_inc(a_ready, 1)

                def scan(c):
                    o, n = chunk(c)
                    pe.wait_ge(w_done, g * NCH + c + 1)
                    pe.wait_ge(xe_done, g * NCH + c + 1)
                    if c == NT:
                        alone(pe)
                    for h in range(HG):
                        pe.matmul(A[2][0:n, h * 64:h * 64 + 64], dec[c % 2][0:n, h, 0:n], xtok[0:n, h * 64:h * 64 + 64],
                                  start=True, stop=True)
                    if c == NT:
                        return
                    if c:
                        pe.wait_ge(d_step, g * DSUM + sum(DSTEPS[:c]))
                        pe.matmul(A[3][:, :], bc[:, 1, o:o + n], st[:, :], start=True, stop=True)
                    pe.matmul(A[4][:, :], bcb[:, 0:P], xe[:, :], start=True, stop=True).then_inc(b_ready, 1)

                def y_back(c):
                    o, n = chunk(c)
                    pe.wait_ge(d_step, g * DSUM + sum(DSTEPS[:c + 1]))
                    if c < NT:
                        pe.wait_ge(a_copied, g * 2 * NCH + 2 * (c + 2))
                    else:
                        alone(pe)
                    for m in range(XT):
                        mm = pe.transpose(A[0][:, m * n:(m + 1) * n], ytok[0:n, m * P:(m + 1) * P], ident[0:n, 0:n])
                    mm.then_inc(y_ready, 1)

                for i in range(3):
                    z_part(i)
                by_token(0)
                for c in range(NCH):
                    z_part(3 + c)
                    if c:
                        y_back(c - 1)
                    scan(c)
                    if c + 1 < NCH:
                        by_token(c + 1)
                pe.wait_ge(cmbm, g * 3 + 3)
                for hp in range(4):
                    pe.wait_ge(s0_in[hp % 2], g * 32 + 16 * (hp // 2) + 16)
                    if hp:
                        pe.wait_ge(s0_new, g * 12 + 3 * hp)
                    for b in range(DB):
                        mm = pe.transpose(A[1 + 3 * (b // 4)][:, (b % 4) * P:(b % 4 + 1) * P], s0[hp % 2][:, b, :], ident[:, :])
                    mm.then_inc(s0_tr, 1)
                    pe.wait_ge(s0t_dve, g * 4 + hp + 1)
                    pe.wait_ge(s0t_act, g * 4 + hp + 1)
                    for b in range(DB):
                        pe.matmul(A[3][0:NS, hp * P:(hp + 1) * P], cm[:, b * NS:(b + 1) * NS], s0t[:, b, :],
                                  start=b == 0, stop=b == DB - 1)
                    for i in range(2):
                        mm = pe.matmul(A[1 + 3 * i][:, :], xe[0:NS, hp * P:(hp + 1) * P],
                                       bm[:, 4 * i:4 * i + 4, :].rearrange("p b n -> p (b n)"), start=True, stop=True)
                    mm.then_inc(s0_up, 1)
                y_back(NT)
                pe.wait_ge(s0_new, g * 12 + 12)
                for m in range(XT):
                    mm = pe.transpose(A[4][:, m * P:(m + 1) * P], st[:, m * P:(m + 1) * P], ident[:, :])
                mm.then_inc(st_ready, 1)
                for f in range(XT):
                    pe.wait_ge(sq_ready, g * XT + (KD + f + 1))
                    for c in range(3):
                        if f == 0:
                            bank(c, use(11))
                        mm = pe.matmul(gap(c), ones[:, :], cols(sq[f % 2], c), start=f == 0, stop=f == XT - 1)
                        if f == XT - 1:
                            mm.then_inc(g_ready[c], 1)
                        elif c == 2:
                            mm.then_inc(sq_used, 1)
                for m in range(KD):
                    for c in range(3):
                        if m == 0:
                            pe.wait_ge(yL_ready, g * 3 * XT + XT * (c + 1) + 1)
                        tile(10 + m, yH, yL, XT, use(12 + m), only=c)
            for s in (vt_out, s_min, pt_out, ob_out):
                pe.sem_inc(s, 2)
            pe.sem_inc(sc_done, 1)

            def qkv_part(j, gr, i):
                k, c = i // 3, i % 3
                if c == 0:
                    pe.wait_ge(w_split, j * 9 + (C_ATT + gr * 3 + k + 2))
                product(c, j * 9 + (U_ATT + gr * 3 + k + 1), (C_ATT + k) % SPL, KD, P, 0, P, hH, hL)

            def unit(j, gr, nxt):
                n = j * 24 + 8 * gr
                qT, kT, vT = qkv[gr]
                for i in range(NT + 2):
                    if i < NT:
                        if i == 0:
                            for c in range(3):
                                pe.wait_ge(g_free[c], j * 9 + (U_ATT + gr * 3 + 3))
                        pe.wait_ge(vt_out, n + i + 2)
                        mm = pe.transpose(A[0][:, 0:P], tokens(vT, gr, i), ident[:, :])
                        if k_tile(gr, i) is not None:
                            mm = pe.transpose(A[0][:, P:2 * P], tokens(kT, gr, i), ident[:, :])
                        mm.then_inc(vt_ready, 1)
                        pe.wait_ge(s_min, n + i + 2)
                        w = P * len(blocks(gr, i))
                        for s in range(2):
                            rows = slice(64 * s, 64 * s + 64)
                            mm = pe.matmul(A[1 + s][:, 0:w], tokens(qT, gr, i)[rows], keys(kT, gr, i)[rows],
                                           start=True, stop=True)
                        mm.then_inc(s_ready, 1)
                    if nxt is not None and i <= NT:
                        qkv_part(*nxt, i)
                    if 1 <= i <= NT:
                        nb = len(blocks(gr, i - 1))
                        pe.wait_ge(p_done, n + i)
                        pe.wait_ge(pt_out, n + i + 1)
                        for s in range(2):
                            for b in range(nb):
                                o = (s * nb + b) * P
                                mm = pe.transpose(A[3][:, o:o + P], sbuf[(i - 1) % 2][:, s, b * P:(b + 1) * P], ident[:, :])
                        mm.then_inc(pt_ready, 1)
                    if i >= 2:
                        bl = blocks(gr, i - 2)
                        pe.wait_ge(pt_out, n + i + 1)
                        pe.wait_ge(vt_out, n + i + 1)
                        pe.wait_ge(ob_out, n + i)
                        for s in range(2):
                            for b, t in enumerate(bl):
                                mm = pe.matmul(A[4][:, 64 * s:64 * s + 64],
                                               pt[i % 2][:, s * len(bl) + b, :], vtok[gr][:, t, 64 * s:64 * s + 64],
                                               start=b == 0, stop=b == len(bl) - 1)
                        mm.then_inc(pv_ready, 1)

            for i in range(9):
                qkv_part(0, 0, i)
            with pe.Fori(0, NJ - 1) as j:
                unit(j, 0, (j, 1))
                unit(j, 1, (j, 2))
                unit(j, 2, (j + 1, 0))
            unit(NJ - 1, 0, (NJ - 1, 1))
            unit(NJ - 1, 1, (NJ - 1, 2))
            unit(NJ - 1, 2, None)
            def gate_tiles(b):
                for k in range(2):
                    pe.wait_ge(w_split, b * 2 + (C_GATE + k + 2))
                    for c in range(3):
                        product(c, b * 3 + (U_SAM + 1 + k), (C_GATE + k) % SPL, KD, P, 0, P, hH, hL)

            gate_tiles(0)
            pe.wait_ge(ob_out, NG * NJ * NT + 2)
            for j in range(NJ):
                pe.wait_ge(mg, 11 * j + 11)
                if j >= 2:
                    pe.wait_ge(aL_ready, 2 * (j - 1))
                for i in range(NT):
                    mm = pe.transpose(A[2 * (j % 2) + i // 4][:, (i % 4) * P:(i % 4 + 1) * P], mb[j % 2][:, i, 0, 0:P], ident[:, :])
                mm.then_inc(mt_ready, 1)
            pe.wait_ge(aL_ready, 2 * NJ)
            for gr in range(NG):
                if gr:
                    pe.wait_ge(kvn_ev, 2 * gr)
                for kv in range(2):
                    for j in range(NJ):
                        mm = pe.transpose(A[kv][0:NS, j * P:(j + 1) * P], qkvs[:, 1 + kv, gr, j, :], ident[:, :])
                mm.then_inc(kvn_ps, 1)
            pe.wait_ge(kvn_ev, 2 * NG)

            def scores(b):
                first = isinstance(b, int)

                def keys_of(j):
                    for i, tiles in enumerate((range(0, 4), range(4, 8), (8,))):
                        f = 3 * j + i
                        g = f - 4 if f >= 4 else f + 8
                        back = 0 if f >= 4 else 1
                        if f >= 4 or not first:
                            if g % 3 == 0:
                                pe.wait_ge(kt_dve, b * 4 + (g // 3 + 1 - 4 * back))
                            else:
                                pe.wait_ge(kt_act, b * 8 + (2 * (g // 3) + g % 3 - 8 * back))
                        for t in tiles:
                            mm = pe.transpose(A[f % 4][:, (t % 4) * P:(t % 4 + 1) * P], kraw[:, t, j * P:(j + 1) * P], ident[:, :])
                        mm.then_inc(k_fill, 1)

                def against(j):
                    pe.wait_ge(kt_dve, b * 4 + j + 1)
                    pe.wait_ge(kt_act, b * 8 + 2 * j + 2)
                    if j == 0:
                        pe.wait_ge(qb_ready, b + 1)
                        for c in range(3):
                            bank(c, b * 3 + (U_SAM + 3))
                    k = ktr[j % 2]
                    pe.matmul(G[0][0:NS, 0:P], qblk[:, 0, j, :], k[:, 0:P], start=j == 0, stop=j == NJ - 1, skip_group_check=True)
                    for gr in range(NG):
                        mm = pe.matmul(G[0][0:NS, P + DS * gr:P + DS * gr + DS], qblk[:, gr, j, :], qkvs[:, 1, gr, j, ds(b * DS, DS)],
                                       start=False, stop=j == NJ - 1, skip_group_check=True)
                    if j == NJ - 1:
                        mm.then_inc(g_ready[0], 1)
                    m1 = pe.matmul(G[1][0:NS, :], qblk[:, 1, j, :], k[:, P:P + 512], start=j == 0, stop=j == NJ - 1)
                    if j == NJ - 1:
                        m1.then_inc(g_ready[1], 1)
                    m2_ = pe.matmul(G[2][0:NS, :], qblk[:, 2, j, :], k[:, P + 512:P + 1024], start=j == 0, stop=j == NJ - 1)
                    if j == NJ - 1:
                        m2_.then_inc(g_ready[2], 1)
                    else:
                        m2_.then_inc(sc_done, 1)

                pe.wait_ge(k_in, b * 96 + 96)
                keys_of(0)
                for j in range(NJ):
                    if j + 1 < NJ:
                        keys_of(j + 1)
                    against(j)
                pe.drain().then_inc(sc_done, 1)

            def values(b):
                pe.wait_ge(sm_dve, b * 3 + 3)
                alone(pe)
                offs = [0] + [152 + P * t for t in range(8)]
                for t, o in enumerate(offs):
                    pe.transpose(A[t // 8][:, (t % 8) * NS:(t % 8 + 1) * NS], sS[:, o:o + P], ident[0:NS, 0:NS])
                pe.transpose(A[1][0:24, NS:2 * NS], sS[:, P:P + 24], ident[0:NS, 0:NS]).then_inc(sp_ready, 1)
                pe.wait_ge(spt_dve, b + 1)
                pe.wait_ge(spt_act, b + 1)
                pe.wait_ge(v_in, b * 144 + 144)
                if not (isinstance(b, int) and b == 0):
                    pe.wait_ge(aS_out, b + 1)
                for j in range(NJ):
                    for t in range(9):
                        pe.matmul(A[4][:, 16 * j:16 * j + 16], vraw[:, t, j * P:(j + 1) * P], pts[:, t, 16 * j:16 * j + 16],
                                  start=t == 0, stop=False)
                    mm = pe.matmul(A[4][:, 16 * j:16 * j + 16], vnew[:, j * P:(j + 1) * P], pts[0:24, 9, 16 * j:16 * j + 16],
                                   start=False, stop=True)
                mm.then_inc(spv_ready, 1)

            pe.sem_inc(aS_out, 1)

            scores(0)
            with pe.Fori(0, DB - 1) as b:
                gate_tiles(b + 1)
                scores(b + 1)
                values(b)
            values(DB - 1)

            pe.wait_ge(aL_ready, 2 * NJ + 1)
            for m in range(KD):
                pe.wait_ge(w_split, C_PROJ + m + 2)
                for c in range(3):
                    product(c, U_PROJ + m + 1, (C_PROJ + m) % SPL, NJ, P, 0, P, aH, aL)
            for m in range(KD):
                pe.wait_ge(w_split, C_OUT + m + 2)
                for c in range(3):
                    if m == 0:
                        pe.wait_ge(hL_ready, 24 + KD * (c + 1))
                    product(c, U_OUT + m + 1, (C_OUT + m) % SPL, KD, P, 0, P, hH, hL)
            sums(KD, U_NORME, 24)
            sums(KD, U_NORMF, 32)

            def up(n, u, n0, first=False):
                for i in range(4):
                    pe.wait_ge(w_split, n + i + 2)
                    for c in range(3):
                        if first and i == 0:
                            pe.wait_ge(hL_ready, 48 + KD * (c + 1))
                        product(c, u + i + 1, (n0 + i) % SPL, KD, P, 0, P, hH, hL)

            def down(n, u, n0, k, par):
                pe.wait_ge(uL_ready, k * 2 + 4)
                for i in range(2):
                    pe.wait_ge(w_split, n + i + 2)
                    for m in range(4):
                        for c in range(3):
                            product(c, u + 4 * i + m + 1, (n0 + i) % SPL, 2, 512, m * P, P, uH[par], uL[par])

            up(C_FF, U_FF, C_FF, first=True)
            with pe.Fori(0, 5) as i:
                up(i * 12 + (C_FF + 4), i * 24 + (U_FF + 4), C_FF + 4)
                down(i * 12 + (C_FF + 8), i * 24 + (U_FF + 8), C_FF + 8, i * 2, 0)
                up(i * 12 + (C_FF + 10), i * 24 + (U_FF + 16), C_FF + 10)
                down(i * 12 + (C_FF + 14), i * 24 + (U_FF + 20), C_FF + 14, i * 2 + 1, 1)
            down(C_FF + 64, U_FF + 124, C_FF + 64, 10, 0)
            sums(KD, U_NORML, 40)
            pe.wait_ge(ncb_in, 16)
            for q in range(6):
                if q:
                    pe.wait_ge(nct_ev, q)
                for t in range(4):
                    mm = pe.transpose(A[4][0:27, t * P:(t + 1) * P], ncb[:, 4 * q + t, :], ident[:, :])
                mm.then_inc(nct_ready, 1)
            for t in range(9):
                o, r = (t * P, P) if t < NT else (SEQ, NS)
                pe.wait_ge(y_done, 2 * KD * (1 + sum(hi < o + r for _, hi in TH)))
                if t >= 2:
                    pe.wait_ge(yo_act, t - 1)
                    pe.wait_ge(yo_dve, t - 1)
                for f in range(KD):
                    mm = pe.transpose(A[2 * (t % 2) + f // 4][0:r, (f % 4) * P:(f % 4 + 1) * P], x1[:, f, o:o + r], ident[:, :])
                mm.then_inc(yt_ready, 1)


_INS = ['x_prompt', 'x_sample', 'cache_kv_w128', 'cache_kv_w512', 'cache_kv_w2048', 'state_conv', 'state_ssm',
        'pre_mix_norm', 'w_in', 'conv_w', 'conv_b', 'dt_bias', 'a_log', 'd_skip', 'ssd_norm', 'w_attn_out',
        'w_ssd_out', 'w_out', 'post_mix_norm', 'pre_ffn_norm', 'w_up', 'w_down', 'post_ffn_norm']
_OUTS = ([(1, SEQ, D), (DB, DS, D)] + [(1, 1, min(w, SEQ), 2, HEADS, E_) for w, _ in GROUPS]
         + [(1, 1, CW - 1, CONVD), (1, 1, SH, 64, NST)] + [(1, DB, r, 2, HEADS, E_) for r in ROWS]
         + [(1, DB, CW - 1, CONVD), (1, DB, SH, 64, NST)])


def kernel(**inputs):
    import numpy as _np
    import concourse.bacc as _bacc
    from concourse import mybir as _mybir
    from concourse.bass_utils import run_bass_kernel_spmd as _run

    nc = _bacc.Bacc("TRN2", target_bir_lowering=False, num_devices=1, dynamic_dma_scratch_size=1024)
    arrays, args = {}, []
    for name in _INS:
        a = _np.ascontiguousarray(inputs[name])
        arrays[f"in_{name}_dram"] = a
        args.append(nc.dram_tensor(f"in_{name}_dram", a.shape, _mybir.dt.from_np(a.dtype), kind="ExternalInput").ap())
    for i, shape in enumerate(_OUTS):
        args.append(nc.dram_tensor(f"out_{i}_dram", shape, _mybir.dt.float32, kind="ExternalOutput").ap())
    trunk(nc, *args)
    r = _run(nc, [arrays], core_ids=[0])
    return tuple(r.results[0][f"out_{i}_dram"] for i in range(len(_OUTS)))
```
